# Optimizing a Trainium2 kernel written in Bass

```python
import jax, jax.numpy as jnp
from jax import lax
import numpy as np

D_MODEL = 1024
BATCH = 1
SEQ = 512
DEPTH = 2

PLE_DIM = 256
EPS = 1e-6
N_EVEN = (DEPTH + 1) // 2
N_ODD = DEPTH // 2

A_WIDTH = D_MODEL // 2
A_HEADS = 4
A_DK = A_WIDTH // A_HEADS
A_DV = A_WIDTH // A_HEADS
A_CHUNK = 32
B_WIDTH = D_MODEL // 2
CONV_W = 3
AB_IN = 4 * A_WIDTH + 3 * B_WIDTH
AB_SPLITS = (A_WIDTH, 2 * A_WIDTH, 3 * A_WIDTH, 4 * A_WIDTH,
             4 * A_WIDTH + B_WIDTH, 4 * A_WIDTH + 2 * B_WIDTH)
C_HEAD_DIM = 64
C_Q_HEADS = D_MODEL // C_HEAD_DIM
C_KV_HEADS = 2
C_GROUP = C_Q_HEADS // C_KV_HEADS
WINDOW = 128
C_BLOCK = WINDOW
C_IN = (C_Q_HEADS + 2 * C_KV_HEADS) * C_HEAD_DIM
N_EXPERTS = 16
N_GROUPS = 4
EXPERTS_PER_GROUP = N_EXPERTS // N_GROUPS
TOP_K = 2
D_EXPERT = 512

kernel_name = "hybrid_hgrn2_shortconv_swa_sink_grouped_moe"

def rms_norm(x, g):
    x32 = x.astype(jnp.float32)
    y = x32 * lax.rsqrt(jnp.mean(x32 * x32, axis=-1, keepdims=True) + EPS)
    return (y * g.astype(jnp.float32)).astype(x.dtype)

def hgrn2_chunkwise(q, k, v, log_f):
    bsz, t, h, _ = q.shape
    n = t // A_CHUNK

    def to_chunks(a):
        return a.reshape(bsz, n, A_CHUNK, h, a.shape[-1]).transpose(1, 0, 3, 2, 4)

    q, k, v, log_f = map(to_chunks, (q, k, v, log_f))
    b = jnp.cumsum(log_f, axis=3)
    b_last = b[:, :, :, -1, :]
    q_dec = q * jnp.exp(b)
    k_inv = k * jnp.exp(-b)
    k_tail = k * jnp.exp(b_last[:, :, :, None, :] - b)
    causal = jnp.tril(jnp.ones((A_CHUNK, A_CHUNK), jnp.float32))
    scores = jnp.einsum('nbhid,nbhjd->nbhij', q_dec, k_inv) * causal
    o_intra = jnp.einsum('nbhij,nbhjv->nbhiv', scores, v)

    def step(state, xs):
        q_c, k_c, v_c, decay = xs
        o_c = jnp.einsum('bhid,bhdv->bhiv', q_c, state)
        state = state * decay[..., None] + jnp.einsum('bhjd,bhjv->bhdv', k_c, v_c)
        return state, o_c

    s0 = jnp.zeros((bsz, h, q.shape[-1], v.shape[-1]), jnp.float32)
    _, o_inter = lax.scan(step, s0, (q_dec, k_tail, v, jnp.exp(b_last)))
    o = o_intra + o_inter
    return o.transpose(1, 0, 3, 2, 4).reshape(bsz, t, h, v.shape[-1])

def causal_depthwise_conv(y, w):
    return lax.conv_general_dilated(
        y, w[:, None, :].astype(y.dtype), window_strides=(1,),
        padding=[(CONV_W - 1, 0)], dimension_numbers=('NWC', 'WIO', 'NWC'),
        feature_group_count=y.shape[-1])

def hgrn2_shortconv_mixer(u, w_in, lb, out_norm, conv_w, w_out):
    bsz, t, _ = u.shape
    z = u @ w_in
    q, f, inp, g, gate_b, gate_c, h_b = jnp.split(z, AB_SPLITS, axis=-1)

    def heads(a):
        return a.reshape(bsz, t, A_HEADS, -1)

    forget = lb + (1.0 - lb) * jax.nn.sigmoid(f.astype(jnp.float32))
    o_a = hgrn2_chunkwise(heads(jax.nn.silu(q.astype(jnp.float32))),
                          heads(1.0 - forget),
                          heads(inp.astype(jnp.float32)),
                          heads(jnp.log(forget)))
    o_a = rms_norm(o_a, out_norm) * jax.nn.sigmoid(heads(g.astype(jnp.float32)))
    o_a = o_a.reshape(bsz, t, A_WIDTH).astype(u.dtype)
    o_b = gate_b * causal_depthwise_conv(gate_c * h_b, conv_w)
    return jnp.concatenate([o_a, o_b], axis=-1) @ w_out

def swa_sink_attention(u, w_in, b_in, sinks, w_out, b_out):
    bsz, t, _ = u.shape
    nb = t // C_BLOCK
    z = u @ w_in + b_in
    q, k, v = jnp.split(z, [C_Q_HEADS * C_HEAD_DIM, (C_Q_HEADS + C_KV_HEADS) * C_HEAD_DIM], axis=-1)
    q = q.reshape(bsz, nb, C_BLOCK, C_KV_HEADS, C_GROUP, C_HEAD_DIM)
    k = k.reshape(bsz, nb, C_BLOCK, C_KV_HEADS, C_HEAD_DIM)
    v = v.reshape(bsz, nb, C_BLOCK, C_KV_HEADS, C_HEAD_DIM)

    def with_prev(a):
        prev = jnp.concatenate([jnp.zeros_like(a[:, :1]), a[:, :-1]], axis=1)
        return jnp.concatenate([prev, a], axis=2)

    kk, vv = with_prev(k), with_prev(v)
    scale = C_HEAD_DIM ** -0.5
    s = jnp.einsum('bnqkgd,bnskd->bkgnqs', q, kk).astype(jnp.float32) * scale
    qi = jnp.arange(C_BLOCK)[:, None] + C_BLOCK
    si = jnp.arange(2 * C_BLOCK)[None, :]
    rel = qi - si
    band = (rel >= 0) & (rel < WINDOW)
    real = (jnp.arange(nb)[:, None, None] > 0) | (si[None] >= C_BLOCK)
    mask = band[None] & real
    s = jnp.where(mask, s, -jnp.inf)
    sink = sinks.astype(jnp.float32).reshape(C_KV_HEADS, C_GROUP)[None, :, :, None, None, None]
    m = jnp.maximum(jnp.max(s, axis=-1, keepdims=True), sink)
    e = jnp.exp(s - m)
    probs = e / (jnp.sum(e, axis=-1, keepdims=True) + jnp.exp(sink - m))
    o = jnp.einsum('bkgnqs,bnskd->bnqkgd', probs.astype(vv.dtype), vv)
    return o.reshape(bsz, t, D_MODEL) @ w_out + b_out

def grouped_moe(v, w_router, w_gate, w_up, w_down):
    bsz, t, d = v.shape
    xt = v.reshape(-1, d)
    scores = jax.nn.softmax((xt @ w_router).astype(jnp.float32), axis=-1)
    grouped = scores.reshape(-1, N_GROUPS, EXPERTS_PER_GROUP)
    group_score = jnp.sum(lax.top_k(grouped, TOP_K)[0], axis=-1)
    sel = jnp.argmax(group_score, axis=-1)
    in_group = jnp.take_along_axis(grouped, sel[:, None, None], axis=1)[:, 0]
    vals, idx = lax.top_k(in_group, TOP_K)
    expert_ids = sel[:, None] * EXPERTS_PER_GROUP + idx
    weights = vals / jnp.sum(vals, axis=-1, keepdims=True)
    combine = jnp.einsum('nk,nke->ne', weights,
                         jax.nn.one_hot(expert_ids, N_EXPERTS, dtype=jnp.float32)).astype(v.dtype)
    y = jnp.zeros_like(xt)
    for e in range(N_EXPERTS):
        hidden = jax.nn.silu(xt @ w_gate[e]) * (xt @ w_up[e])
        y = y + combine[:, e:e + 1] * (hidden @ w_down[e])
    return y.reshape(bsz, t, d)

def setup_inputs(seed: int = 0) -> dict:
    key = jax.random.key(seed)
    ks = jax.random.split(key, 24)

    def nrm(k, shape, scale):
        return jax.random.normal(k, shape, jnp.float32) * scale

    def gain(k, shape):
        return 1.0 + 0.05 * jax.random.normal(k, shape, jnp.float32)

    out_scale = (2 * DEPTH) ** -0.5
    return {
        "x": nrm(ks[0], (BATCH, SEQ, D_MODEL), 1.0),
        "p": nrm(ks[1], (DEPTH, BATCH, SEQ, PLE_DIM), 1.0),
        "norm_mix": gain(ks[2], (DEPTH, D_MODEL)),
        "norm_ffn": gain(ks[3], (DEPTH, D_MODEL)),
        "norm_ple": gain(ks[4], (DEPTH, D_MODEL)),
        "norm_final": gain(ks[5], (D_MODEL,)),
        "w_in_ab": nrm(ks[6], (N_EVEN, D_MODEL, AB_IN), D_MODEL ** -0.5),
        "hgrn_lb_logits": nrm(ks[7], (DEPTH + 1, A_WIDTH), 0.1),
        "hgrn_out_norm": gain(ks[8], (N_EVEN, A_DV)),
        "conv_w": nrm(ks[9], (N_EVEN, CONV_W, B_WIDTH), CONV_W ** -0.5),
        "w_out_ab": nrm(ks[10], (N_EVEN, D_MODEL, D_MODEL), D_MODEL ** -0.5 * out_scale),
        "w_in_c": nrm(ks[11], (N_ODD, D_MODEL, C_IN), D_MODEL ** -0.5),
        "b_in_c": nrm(ks[12], (N_ODD, C_IN), 0.02),
        "sinks": nrm(ks[13], (N_ODD, C_Q_HEADS), 1.0),
        "w_out_c": nrm(ks[14], (N_ODD, D_MODEL, D_MODEL), D_MODEL ** -0.5 * out_scale),
        "b_out_c": nrm(ks[15], (N_ODD, D_MODEL), 0.02),
        "w_router": nrm(ks[16], (D_MODEL, N_EXPERTS), D_MODEL ** -0.5),
        "w_gate_e": nrm(ks[17], (DEPTH, N_EXPERTS, D_MODEL, D_EXPERT), D_MODEL ** -0.5),
        "w_up_e": nrm(ks[18], (DEPTH, N_EXPERTS, D_MODEL, D_EXPERT), D_MODEL ** -0.5),
        "w_down_e": nrm(ks[19], (DEPTH, N_EXPERTS, D_EXPERT, D_MODEL), D_EXPERT ** -0.5 * out_scale),
        "w_ple_gate": nrm(ks[20], (DEPTH, D_MODEL, D_MODEL), D_MODEL ** -0.5),
        "w_ple_proj": nrm(ks[21], (DEPTH, PLE_DIM, D_MODEL), PLE_DIM ** -0.5 * out_scale),
    }

def reference(x, p, norm_mix, norm_ffn, norm_ple, norm_final, w_in_ab, hgrn_lb_logits,
              hgrn_out_norm, conv_w, w_out_ab, w_in_c, b_in_c, sinks, w_out_c, b_out_c,
              w_router, w_gate_e, w_up_e, w_down_e, w_ple_gate, w_ple_proj):
    lower_bounds = jnp.cumsum(jax.nn.softmax(hgrn_lb_logits.astype(jnp.float32), axis=0), axis=0)
    h = x
    for i in range(DEPTH):
        u = rms_norm(h, norm_mix[i])
        j = i // 2
        if i % 2 == 0:
            mix = hgrn2_shortconv_mixer(u, w_in_ab[j], lower_bounds[i], hgrn_out_norm[j],
                                        conv_w[j], w_out_ab[j])
        else:
            mix = swa_sink_attention(u, w_in_c[j], b_in_c[j], sinks[j], w_out_c[j], b_out_c[j])
        h = h + mix
        h = h + grouped_moe(rms_norm(h, norm_ffn[i]), w_router, w_gate_e[i], w_up_e[i], w_down_e[i])
        ple_gate = jax.nn.sigmoid(rms_norm(h, norm_ple[i]) @ w_ple_gate[i])
        h = h + ple_gate * (p[i] @ w_ple_proj[i])
    return rms_norm(h, norm_final)


_drawn_inputs = setup_inputs


def setup_inputs(seed=0):
    import zlib

    import numpy as np

    out = dict(_drawn_inputs(seed))
    spreads = {}
    factors = {'hgrn_lb_logits': 12.223, 'sinks': 8.0, 'norm_ple': 7.624, 'b_in_c': 3.058}
    for name, (base, spread) in spreads.items():
        noise = np.random.default_rng([zlib.crc32(name.encode()), seed]).standard_normal(out[name].shape)
        drawn = base * np.exp(spread * noise) if base else spread * noise
        out[name] = __import__('jax').numpy.asarray(drawn.astype(out[name].dtype))
    for name, factor in factors.items():
        out[name] = (out[name] * factor).astype(out[name].dtype)
    return out
```

```python
import numpy as np
import concourse.bass as bass
from concourse import mybir
from contextlib import ExitStack

P = 128
SEQ, D = 512, 1024
TB = SEQ // P
KT = D // P
LAYERS = 2
AW = D // 2
HEADS, CHUNK = 4, 32
NCH = SEQ // CHUNK
CPB = P // CHUNK
HD, QH, KVH = 64, 16, 2
EXP, GROUPS, EPG = 16, 4, 4
FE = 512
PLE = 256
EPS = 1e-6
SLOTS = 128
PASSES = -(-SEQ // SLOTS) - 1
STEPS = PASSES * EXP
FAR = 4096.0
NEG = -1e30
RAW, SPL = 6, 3
CW = 2048

BLK = {"f": 0, "q": 1, "v": 2, "g": 3, "C": 4, "H": 5, "B": 6, "out0": 7, "ple0": 9,
       "aq": 11, "akv": 13, "out1": 14, "ple1": 16}
MOE_CHUNKS = 6 * EXP
MOE0 = 18
PLE0 = MOE0 + MOE_CHUNKS
ATT = PLE0 + 4
MOE1 = ATT + 9
PLE1 = MOE1 + MOE_CHUNKS
NCHUNKS = PLE1 + 4
MOE = (MOE0, MOE1)


def first_chunk(k):
    if k < 9:
        return 2 * k
    if k < 11:
        return PLE0 + 2 * (k - 9)
    if k < 14:
        return ATT + 2 * (k - 11)
    if k < 16:
        return ATT + 5 + 2 * (k - 14)
    return PLE1 + 2 * (k - 16)


CONST = {}
_at = 0
for _name, _n in (("ident", 128), ("upper", 128), ("iota", 128), ("tok", TB), ("wr", KT * EXP),
                  ("tril", 16), ("eps", 1)):
    CONST[_name] = (_at, _n)
    _at += _n
CONST_N = _at
HCONST = {}
_at = 0
for _name, _n in (("triI", 128), ("triS", 128), ("ind", CPB), ("onorm", 128), ("convw", 12)):
    HCONST[_name] = (_at, _n)
    _at += _n
HCONST_N = _at
ACONST = {}
_at = 0
for _name, _n in (("mask", 512), ("bq", 9), ("bv", 128), ("sink", QH)):
    ACONST[_name] = (_at, _n)
    _at += _n
ACONST_N = _at

AR_F, AR_K, AR_E, AR_Q, AR_V, AR_G = (2048 * i for i in range(6))
AR_XN, AR_GAIN, AR_JUNK = 8192, 10240, 11264
AR_S, AR_ST, AR_YT, AR_ET, AR_HC, AR_DEC = 12288, 12800, 13312, 13824, 14336, 14736
AR_LBL, AR_LB = AR_Q, AR_ST
ARENA = 15360
AR_VT, AR_RT, AR_OH, AR_XG, AR_HID, AR_SG, AR_OUT = 0, 2048, 4096, 4608, 5632, 6144, 6656
AR_PT, AR_PW, AR_PO, AR_YC = 14336, 12288, 4096, 0
AR_SIG = 12288
AR_AC, AR_QT, AR_KT, AR_VN, AR_SM, AR_PR, AR_PTT, AR_AO, AR_ST2, AR_BO = (
    0, 1024, 5120, 5760, 12288, 13312, 6400, 8192, 14336, 2048)


def build(nc, consts, hconsts, aconsts, gains, lbl, bout, x, pT, w_dense, w_moe, w_proj, out,
          vscr, yscr):
    f32, f32r, i32 = mybir.dt.float32, mybir.dt.float32r, mybir.dt.int32
    ALU, ACT = mybir.AluOpType, mybir.ActivationFunctionType
    AX = mybir.AxisListType.X
    ctx = ExitStack()
    with ctx:
        def sb(name, shape, dt=f32):
            return ctx.enter_context(nc.sbuf_tensor(name, shape, dt))

        def sem(name):
            return ctx.enter_context(nc.semaphore(name))

        def sems(name, n):
            return [sem(f"{name}{i}") for i in range(n)]

        h = sb("h", [P, TB, D])
        raw = sb("raw", [P, RAW, CW])
        whi = sb("whi", [P, SPL, CW], f32r)
        wlo = sb("wlo", [P, SPL, CW], f32r)
        ahi = sb("ahi", [P, KT, SEQ], f32r)
        alo = sb("alo", [P, KT, SEQ], f32r)
        ar = sb("arena", [P, ARENA])
        con = sb("con", [P, CONST_N])
        st = sb("st", [P, 7 * TB, 3])
        cur = sb("cur", [P, 4], i32)
        curw = sb("curw", [P, 4])
        ssb = sb("ssb", [P, 4, 8])
        flag = sb("flag", [P, 2], i32)
        psum = ctx.enter_context(nc.psum_tensor("psum", [P, 8, 512], f32))
        PS = [psum[:, i, :] for i in range(8)]

        def c_(name):
            a, n = CONST[name]
            return con[:, a:a + n]

        def hc(name):
            a, n = HCONST[name]
            return ar[:, AR_HC + a:AR_HC + a + n]

        def ac(name):
            a, n = ACONST[name]
            return ar[:, AR_AC + a:AR_AC + a + n]

        def area(at, *shape):
            n = int(np.prod(shape))
            v = ar[:, at:at + n]
            if len(shape) == 2:
                v = v.rearrange("p (a b) -> p a b", a=shape[0])
            if len(shape) == 3:
                v = v.rearrange("p (a b c) -> p a b c", a=shape[0], b=shape[1])
            return v

        ident, upper, iota = c_("ident"), c_("upper"), c_("iota")

        w_full = sems("w_full", RAW)
        hi_ready = sem("hi_ready")
        lo_ready = sem("lo_ready")
        w_used = sem("w_used")
        d_done = sem("d_done")
        s_add = sem("s_add")
        g_H = sem("g_H")
        s_con = sem("s_con")
        s_x = sems("s_x", TB)
        s_hc = sem("s_hc")
        s_acon = sem("s_acon")
        s_gain = sem("s_gain")
        h_ready = sem("h_ready")
        n_root = sem("n_root")
        n_xn = sem("n_xn")
        n_t = sem("n_t")
        n_hi = sem("n_hi")
        n_lo = sem("n_lo")
        f_a = sem("f_a")
        f_v = sem("f_v")
        a_link = sem("a_link")
        v_link = sem("v_link")
        s_rows = sems("s_rows", TB)
        s_y = sems("s_y", 2)

        p_ready = sem("p_ready")

        g_lb = sem("g_lb")
        g_sig, g_k, g_log = sem("g_sig"), sem("g_k"), sem("g_log")
        g_cum = sem("g_cum")
        g_eb, g_enb, g_esf = sem("g_eb"), sem("g_enb"), sem("g_esf")
        g_kinv, g_ktail, g_dec, g_silu, g_qdec = (sem("g_kinv"), sem("g_ktail"), sem("g_dec"),
                                                   sem("g_silu"), sem("g_qdec"))
        g_kqT, g_KT, g_QT = sem("g_kqT"), sem("g_KT"), sem("g_QT")
        g_v, g_g = sem("g_v"), sem("g_g")
        g_sc, g_scm = sem("g_sc"), sem("g_scm")
        g_U, g_in, g_S = sem("g_U"), sem("g_in"), sem("g_S")
        g_o, g_osum, g_oroot, g_oa = sem("g_o"), sem("g_osum"), sem("g_oroot"), sem("g_oa")
        g_C, g_ob = sem("g_C"), sem("g_ob")
        g_oT, g_mhi, g_mlo, g_bhi, g_blo = (sem("g_oT"), sem("g_mhi"), sem("g_mlo"),
                                            sem("g_bhi"), sem("g_blo"))
        t_q, t_v = sem("t_q"), sem("t_v")
        t_pad, t_s, t_neg, t_sub, t_e = (sem("t_pad"), sem("t_s"), sem("t_neg"), sem("t_sub"),
                                         sem("t_e"))
        t_pT, t_pTc, t_pv, t_den, t_o, t_oT, t_hi, t_lo = (
            sem("t_pT"), sem("t_pTc"), sem("t_pv"), sem("t_den"), sem("t_o"), sem("t_oT"),
            sem("t_hi"), sem("t_lo"))
        t_bo = sem("t_bo")
        names = ("rt", "rtd", "ex", "msk", "rk", "oh", "ix", "ixe", "src", "ga", "xt", "xhi",
                 "xlo", "silu", "hid", "hT", "hhi", "hlo", "cw", "ou", "sca", "flg",
                 "pl", "pj", "pe", "sg", "gt", "xz")
        M = [{n: sem(f"m{i}_{n}") for n in names} for i in range(LAYERS)]

        fnames = ("pos",
                  "w",
                  "ga",
                  "sca",
                  "pe",
                  "act",
                  "dve")
        X = [{n: sem(f"x{i}_{n}") for n in fnames} for i in range(LAYERS)]

        def more(eng, layer):
            eng.wait_ge(M[layer]["flg"], 1)
            return eng.If(eng.value_load(flag[0:1, layer:layer + 1], min_val=0, max_val=1) > 0)

        def halves(t):
            return t.bitcast(f32)

        FFN = {1: 0, 4: 1}
        ORDER = {0: 0, 2: 1, 3: 2, 5: 3}

        def nsplit(n, tb, half):
            return (ORDER[n] * TB + tb) * 2 + half + 1

        READ = {1: (g_sig, 0), 2: (g_silu, 0), 3: (g_v, 0), 4: (g_g, 0), 5: (g_C, 0),
                6: (g_H, 0), 7: (g_ob, 0), 8: (s_add, 0), 10: (M[0]["gt"], 0),
                11: (M[0]["gt"], 4), 12: (t_q, 0), 13: (t_q, 4), 15: (s_add, 4),
                17: (M[1]["gt"], 0)}

        def first_key(n):
            return P if n == 0 else 0

        def xn(q):
            return area(AR_XN + q % 2 * D, D)

        RT = {}
        at_ = AR_RT
        for name, shape in (("L", (TB, EXP)), ("ex", (TB, EXP)), ("sc", (TB, EXP)),
                            ("s2", (TB, EXP)), ("in2", (TB, EXP)), ("M", (TB, EXP)),
                            ("w", (TB, EXP)), ("pos", (TB, EXP)), ("rank", (TB, EXP)),
                            ("a", (TB, EXP)), ("gs", (TB, GROUPS)), ("gsel", (TB, GROUPS)),
                            ("grank", (TB, GROUPS)), ("rgs", (TB, GROUPS)), ("mx", (TB,)),
                            ("sm", (TB,)), ("rs", (TB,)), ("cnt", (4,)), ("gt", (16, 4, 4)),
                            ("eq", (16, 4, 4)), ("info", (TB, EXP * 4)), ("ones", (P,)),
                            ("idx", (EXP * 4,))):
            RT[name] = (at_, shape)
            at_ += int(np.prod(shape))

        def rtv(name):
            a, shape = RT[name]
            return area(a, *shape)

        def ones():
            return rtv("ones")

        block = ctx.enter_context(nc.Block())

        def group_done(eng, k, q):
            if q < 3:
                eng.wait_ge(d_done, 3 * k + q + 1)
            else:
                eng.wait_ge(w_used, first_chunk(k) + (1 if k == 13 else 2))

        @block.sync
        def _(sp):
            def load(c, src):
                if c >= RAW:
                    sp.wait_ge(lo_ready, c - RAW + 1)
                sp.dma_start(raw[:, c % RAW, :], src).then_inc(w_full[c % RAW], 16)

            sp.dma_start(con[:, :], consts).then_inc(s_con, 16)
            for tb in range(TB):
                sp.dma_start(h[:, tb, :], x[tb * P:(tb + 1) * P, :]).then_inc(s_x[tb], 16)
            d = 0
            for c in range(MOE0):
                load(c, w_dense[d])
                d += 1
            for layer in range(LAYERS):
                m = M[layer]
                B = MOE[layer]
                for i in range(4):
                    load(B + i, w_moe[layer][i])
                with sp.Fori(0, EXP - 1) as e:
                    for i in range(6):
                        slot = (B + 4 + i) % RAW
                        sp.wait_ge(lo_ready, 6 * e + (B + 4 + i - RAW + 1))
                        sp.dma_start(raw[:, slot, :], w_moe[layer][6 * e + (6 + i if i < 4 else i)])\
                          .then_inc(w_full[slot], 16)
                for i in range(2):
                    load(B + 6 * EXP - 2 + i, w_moe[layer][6 * EXP - 2 + i])
                with more(sp, layer):
                    f = X[layer]
                    sp.wait_ge(lo_ready, B + MOE_CHUNKS)
                    with sp.Fori(0, PASSES) as j:
                        with sp.Fori(0, EXP) as e:
                            sp.wait_ge(f["dve"], 5 * (j * EXP + e) + 1)
                            for i in range(6):
                                sp.dma_start(raw[:, i, :], w_moe[layer][6 * e + i])\
                                  .then_inc(f["w"], 16)
                    sp.wait_ge(f["w"], 96 * STEPS)
                    sp.wait_ge(f["pe"], 5 * STEPS)
                last = (ATT - PLE0 + 9) if layer == 0 else 4
                for c in range(B + MOE_CHUNKS, B + MOE_CHUNKS + last):
                    load(c, w_dense[d])
                    d += 1

        @block.tensor
        def _(pe):
            def mm(o, l, r, start, stop, **kw):
                return nc.tensor.matmul(o, l, r, start=start, stop=stop, **kw)

            def dense(k, lhs, tiles=(0, 4), before=None, after=None):
                for i in range(2):
                    c = first_chunk(k) + i
                    pe.wait_ge(lo_ready, c + 1)
                    s = c % SPL
                    for q in range(4):
                        if i == 0:
                            bank_read(k, q)
                        if before:
                            before(i, q)
                        for t in range(4):
                            kt = tiles[i] + t
                            if lhs == "act":
                                col = slice(t * 512, (t + 1) * 512)
                                a = (ahi[:, kt, q * P:(q + 1) * P], whi[:, s, col])
                                b = (ahi[:, kt, q * P:(q + 1) * P], wlo[:, s, col])
                                e = (alo[:, kt, q * P:(q + 1) * P], whi[:, s, col])
                            else:
                                col = slice(t * 512 + q * P, t * 512 + (q + 1) * P)
                                a = (whi[:, s, col], ahi[:, kt, :])
                                b = (whi[:, s, col], alo[:, kt, :])
                                e = (wlo[:, s, col], ahi[:, kt, :])
                            mm(PS[q][:, :], *a, i == 0 and t == 0, False)
                            mm(PS[q][:, :], *b, False, False)
                            last = mm(PS[q][:, :], *e, False, i == 1 and t == 3)
                        if q == 3:
                            last.then_inc(w_used, 1)
                        elif i == 1:
                            last.then_inc(d_done, 1)
                        if after:
                            after(i, q)

            def bank_read(k, q):
                if k in READ:
                    pe.wait_ge(READ[k][0], READ[k][1] + q + 1)

            def norm_T(n, tb):
                q = n * TB + tb
                pe.wait_ge(n_xn, q + 1)
                for half in range(2):
                    if tb > 0 and n in FFN:
                        pe.wait_ge((f_a, f_v)[half], FFN[n] * TB + tb)
                    elif tb > 0:
                        pe.wait_ge(n_lo, nsplit(n, tb - 1, half))
                    elif n == 1:
                        pe.wait_ge(g_mlo, TB)
                    elif n in (2, 5):
                        pe.wait_ge(M[n // 3]["xlo"], 2 * EXP)
                    elif n == 3:
                        pe.wait_ge(n_lo, nsplit(2, TB - 1, 1))
                    elif n == 4:
                        pe.wait_ge(t_neg, 8 * TB)
                    for t in range(4):
                        kt = half * 4 + t
                        last = nc.tensor.transpose(PS[4 + half][:, t * P:(t + 1) * P],
                                                   xn(q)[:, kt * P:(kt + 1) * P], ident)
                    last.then_inc(n_t, 1)

            pe.wait_ge(s_con, 16)
            for tb in range(2):
                norm_T(0, tb)

            def wait_norm(n):
                def w(i, q):
                    if i == 0:
                        pe.wait_ge(n_lo, nsplit(n, q, 1))
                return w

            def late_T(n):
                return lambda i, q: norm_T(n, q + 2) if i == 0 and q < 2 else None

            dense(BLK["f"], "act", before=wait_norm(0), after=late_T(0))

            def cum(tb):
                pe.wait_ge(g_log, tb + 1)
                if tb == 0:
                    pe.wait_ge(s_hc, 32)
                if tb > 0:
                    pe.wait_ge(g_enb, tb)
                    pe.wait_ge(g_esf, tb)
                F = area(AR_F, TB, 512)
                mm(PS[4][:, :], hc("triI"), F[:, tb, :], True, True)
                mm(PS[5][:, :], hc("triS"), F[:, tb, :], True, True)
                for hh in range(HEADS):
                    at = (tb * HEADS + hh) * CPB
                    last = mm(PS[6][:, at:at + CPB], F[:, tb, hh * P:(hh + 1) * P], hc("ind"),
                              True, True)
                last.then_inc(g_cum, 1)

            def kq_T(tb):
                pe.wait_ge(g_kinv, tb + 1)
                pe.wait_ge(g_qdec, tb + 1)
                if tb == 0:
                    pe.wait_ge(g_dec, 1)
                else:
                    pe.wait_ge(g_KT, tb)
                    pe.wait_ge(g_QT, tb)
                for bank, at in ((7, AR_F), (6, AR_Q)):
                    for hh in range(HEADS):
                        last = nc.tensor.transpose(PS[bank][:, hh * P:(hh + 1) * P],
                                                   area(at, TB, 512)[:, tb, hh * P:(hh + 1) * P],
                                                   ident)
                    last.then_inc(g_kqT, 1)

            dense(BLK["q"], "act", after=lambda i, q: cum(q) if i == 1 else None)
            dense(BLK["v"], "act", after=lambda i, q: kq_T(q) if i == 1 else None)
            dense(BLK["g"], "act")

            KT_, QT_ = area(AR_F, TB, 512), area(AR_Q, TB, 512)
            Kt, V = area(AR_K, TB, 512), area(AR_V, TB, 512)
            S, ST = area(AR_S, HEADS, P), area(AR_ST, HEADS, P)

            def scores(tb):
                if tb == 0:
                    pe.wait_ge(g_KT, TB)
                    pe.wait_ge(g_QT, TB)
                    pe.wait_ge(g_v, TB)
                    pe.wait_ge(g_ktail, TB)
                else:
                    pe.wait_ge(g_scm, tb)
                for hh in range(HEADS):
                    last = mm(PS[4][:, hh * P:(hh + 1) * P], KT_[:, tb, hh * P:(hh + 1) * P],
                              QT_[:, tb, hh * P:(hh + 1) * P], True, True)
                last.then_inc(g_sc, 1)

            def intra(tb):
                pe.wait_ge(g_scm, tb + 1)
                if tb > 0:
                    pe.wait_ge(g_o, tb)
                for hh in range(HEADS):
                    mm(PS[7][:, hh * P:(hh + 1) * P], ST[:, hh, :],
                       V[:, tb, hh * P:(hh + 1) * P], hh == 0, False, skip_group_check=True)

            def chunk(n):
                tb, c = n // CPB, n % CPB
                rows = slice(c * CHUNK, (c + 1) * CHUNK)
                if n >= 2:
                    pe.wait_ge(g_S, n)
                if n < NCH - 1:
                    for hh in range(HEADS):
                        last = mm(PS[5 + n % 2][:, hh * P:(hh + 1) * P],
                                  Kt[rows, tb, hh * P:(hh + 1) * P],
                                  V[rows, tb, hh * P:(hh + 1) * P], True, True)
                    last.then_inc(g_U, 1)
                if n > 0:
                    pe.wait_ge(g_S, n + 1)
                for hh in range(HEADS):
                    last = mm(PS[7][rows, hh * P:(hh + 1) * P],
                              QT_[:, tb, hh * P + c * CHUNK:hh * P + (c + 1) * CHUNK],
                              S[:, hh, :], False, c == CPB - 1 and hh == HEADS - 1,
                              skip_group_check=True)
                last.then_inc(g_in, 1)

            def rec(s):
                tb, r = s // 5, s % 5
                if tb >= TB:
                    return
                if r == 0:
                    scores(tb)
                    return
                if r == 1:
                    intra(tb)
                chunk(tb * CPB + r - 1)

            pe.wait_ge(g_S, 1)
            for b, name in enumerate("CHB"):
                dense(BLK[name], "w", after=lambda i, q, b=b: rec(b * 8 + i * 4 + q))

            def oa_T(tb):
                pe.wait_ge(g_oa, tb + 1)
                if tb >= 2:
                    pe.wait_ge(g_mlo, tb - 1)
                for hh in range(HEADS):
                    last = nc.tensor.transpose(PS[4 + tb % 2][:, hh * P:(hh + 1) * P],
                                               area(AR_G, TB, 512)[:, tb, hh * P:(hh + 1) * P],
                                               ident)
                last.then_inc(g_oT, 1)

            for tb in range(2):
                oa_T(tb)

            def out_before(k):
                def w(i, q):
                    if i == 0 and q == 0 and k == BLK["out0"]:
                        pe.wait_ge(g_blo, 4)
                    if i == 0 and q >= 2 and k == BLK["out0"]:
                        oa_T(q)
                    if i == 1 and k == BLK["out0"]:
                        pe.wait_ge(g_mlo, q + 1)
                return w

            def router(tb):
                m = M[layer]
                pe.wait_ge(f_a, layer * TB + tb + 1)
                pe.wait_ge(f_v, layer * TB + tb + 1)
                for kt in range(KT):
                    last = mm(PS[6][:, tb * EXP:(tb + 1) * EXP],
                              area(AR_VT, 2, KT, P)[:, tb % 2, kt, :],
                              c_("wr")[:, kt * EXP:(kt + 1) * EXP], kt == 0, kt == KT - 1)
                last.then_inc(m["rt"], 1)

            def moe():
                m = M[layer]
                B = MOE[layer]
                MK = rtv("M")
                pe.wait_ge(m["msk"], 1)
                flat = MK.rearrange("p a b -> p (a b)")
                mm(PS[7][:, 0:TB * EXP], upper, flat, True, False, skip_group_check=True)
                for t in range(1, TB):
                    last = mm(PS[7][:, t * EXP:TB * EXP], ones(), flat[:, 0:(TB - t) * EXP],
                              False, t == TB - 1, skip_group_check=True)
                last.then_inc(m["rk"], 1)
                for t in range(TB):
                    last = mm(PS[6][:, 64:64 + EXP], ones(), MK[:, t, :], t == 0, t == TB - 1)
                last.then_inc(m["rk"], 1)

                def index(e):
                    pe.wait_ge(m["oh"], e + 1)
                    pe.wait_ge(m["ixe"], e + 1)
                    OH, info = area(AR_OH, TB, P), rtv("info")
                    for t in range(TB):
                        last = mm(PS[7][:, 0:4], OH[:, t, :],
                                  info[:, t, bass.ds(e * 4, 4)], t == 0, t == TB - 1)
                    last.then_inc(m["ix"], 1)

                def x_T(e):
                    pe.wait_ge(m["ga"], 16 * e + 16)
                    for half in range(2):
                        if isinstance(e, int) and e == 0:
                            pe.wait_ge((f_a, f_v)[half], layer * TB + TB)
                        else:
                            pe.wait_ge(m["xlo"], 2 * e + (half - 1))
                        for t in range(4):
                            kt = half * 4 + t
                            last = nc.tensor.transpose(
                                PS[4 + half][:, t * P:(t + 1) * P],
                                area(AR_XG, D)[:, kt * P:(kt + 1) * P], ident)
                        last.then_inc(m["xt"], 1)

                def up(b, e6, bank):
                    for i in range(2):
                        pe.wait_ge(lo_ready, e6 + (b + i + 1))
                        s = (b + i) % SPL
                        for t in range(4):
                            kt = i * 4 + t
                            w = slice(t * 512, (t + 1) * 512)
                            mm(PS[bank][:, :], ahi[:, kt, 0:P], whi[:, s, w], kt == 0, False)
                            mm(PS[bank][:, :], ahi[:, kt, 0:P], wlo[:, s, w], False, False)
                            last = mm(PS[bank][:, :], alo[:, kt, 0:P], whi[:, s, w], False,
                                      kt == KT - 1)
                        last.then_inc(w_used, 1)

                def down(e, b, e6):
                    pe.wait_ge(m["hlo"], e + 1)
                    pe.wait_ge(m["ou"], 2 * e)
                    for i in range(2):
                        pe.wait_ge(lo_ready, e6 + (b + i + 1))
                        s = (b + i) % SPL
                        for t in range(4):
                            w = slice(t * 512, (t + 1) * 512)
                            mm(PS[2 + i][:, :], ahi[:, t, P:2 * P], whi[:, s, w], t == 0, False)
                            mm(PS[2 + i][:, :], ahi[:, t, P:2 * P], wlo[:, s, w], False, False)
                            last = mm(PS[2 + i][:, :], alo[:, t, P:2 * P], whi[:, s, w], False,
                                      t == 3)
                        last.then_inc(w_used, 1)

                def hid_T(e):
                    pe.wait_ge(m["hid"], e + 1)
                    if not (isinstance(e, int) and e == 0):
                        pe.wait_ge(m["hlo"], e)
                    for t in range(4):
                        last = nc.tensor.transpose(PS[6][:, t * P:(t + 1) * P],
                                                   area(AR_HID, 512)[:, t * P:(t + 1) * P],
                                                   ident)
                    last.then_inc(m["hT"], 1)

                index(0)
                index(1)
                x_T(0)
                pe.wait_ge(h_ready, 3 * layer * TB + TB)

                def step(e, b, e6, prev=True, nx=True, nx2=True):
                    pe.wait_ge(m["xlo"], 2 * e + 2)
                    if prev:
                        pe.wait_ge(m["silu"], e)
                    up(b, e6, 0)
                    if prev:
                        hid_T(e - 1)
                        pe.wait_ge(m["hid"], e)
                    up(b + 2, e6, 1)
                    if nx:
                        x_T(e + 1)
                    if nx2:
                        index(e + 2)
                    if prev:
                        down(e - 1, b + 4, e6)

                step(0, B, 0, prev=False)
                step(1, B - 2 + 6, 0)
                with pe.Fori(2, EXP - 2) as e:
                    step(e, B - 2, 6 * e)
                for e in (EXP - 2, EXP - 1):
                    step(e, B - 2 + 6 * e, 0, nx=e + 1 < EXP, nx2=False)
                hid_T(EXP - 1)
                down(EXP - 1, B + 6 * EXP - 2, 0)
                with more(pe, layer):
                    further(m, X[layer])

            def further(m, f):
                OH, info = area(AR_OH, TB, P), rtv("info")
                pe.wait_ge(m["ou"], 2 * EXP)
                with pe.Fori(0, PASSES) as j:
                    with pe.Fori(0, EXP) as e:
                        t = j * EXP + e
                        pe.wait_ge(f["dve"], 5 * t + 1)
                        for tb in range(TB):
                            last = mm(PS[7][:, 0:4], OH[:, tb, :],
                                      info[:, tb, bass.ds(e * 4, 4)], tb == 0, tb == TB - 1)
                        last.then_inc(f["pe"], 1)
                        pe.wait_ge(f["ga"], 16 * t + 16)
                        for kt in range(KT):
                            last = nc.tensor.transpose(
                                PS[4 + kt // 4][:, kt % 4 * P:(kt % 4 + 1) * P],
                                area(AR_XG, D)[:, kt * P:(kt + 1) * P], ident)
                        last.then_inc(f["pe"], 1)
                        pe.wait_ge(f["act"], 6 * t + 2)
                        pe.wait_ge(f["w"], 96 * t + 96)
                        xT = area(AR_VT, KT, P)
                        for i in range(4):
                            for k in range(4):
                                kt = i % 2 * 4 + k
                                last = mm(PS[i // 2][:, :], xT[:, kt, :],
                                          raw[:, i, k * 512:(k + 1) * 512], kt == 0, kt == KT - 1)
                        last.then_inc(f["pe"], 1)
                        pe.wait_ge(f["dve"], 5 * t + 5)
                        for k in range(4):
                            last = nc.tensor.transpose(PS[6][:, k * P:(k + 1) * P],
                                                       area(AR_HID, 512)[:, k * P:(k + 1) * P],
                                                       ident)
                        last.then_inc(f["pe"], 1)
                        pe.wait_ge(f["act"], 6 * t + 4)
                        for i in range(2):
                            for k in range(4):
                                last = mm(PS[2 + i][:, :], area(AR_VT + D, 4, P)[:, k, :],
                                          raw[:, 4 + i, k * 512:(k + 1) * 512], k == 0, k == 3)
                        last.then_inc(f["pe"], 1)
                pe.wait_ge(f["act"], 6 * STEPS)

            def proj():
                m = M[layer]
                pe.wait_ge(m["pl"], 32)
                for g in range(8):
                    tb, half = g // 2, g % 2
                    if g >= 4:
                        pe.wait_ge(m["pe"], g - 3)
                    elif g == 0:
                        pe.wait_ge(m["ou"], 2 * EXP)
                    for t in range(2):
                        last = mm(PS[g % 4][:, :], area(AR_PT, 2, 512)[:, t, tb * P:(tb + 1) * P],
                                  area(AR_PW, 2, D)[:, t, half * 512:(half + 1) * 512],
                                  t == 0, t == 1)
                    last.then_inc(m["pj"], 1)

            def ple():
                n = 2 + 3 * layer
                k = BLK["ple0"] if layer == 0 else BLK["ple1"]

                def w(i, q):
                    if i == 0:
                        pe.wait_ge(n_lo, nsplit(n, q, 1))
                        if q == 0:
                            pe.wait_ge(M[layer]["pe"], 8)
                dense(k, "act", before=w, after=late_T(n))
                dense(k + 1, "act")
                if layer == 0:
                    for tb in range(TB):
                        norm_T(3, tb)

            def after_out(n):
                def f(i, q):
                    if i == 1 and q > 0:
                        norm_T(n, q - 1)
                        if q > 1:
                            router(q - 2)
                return f

            layer = 0
            dense(BLK["out0"], "act", tiles=(4, 0), before=out_before(BLK["out0"]))
            dense(BLK["out0"] + 1, "act", tiles=(4, 0), after=after_out(1))
            norm_T(1, TB - 1)
            router(TB - 2)
            router(TB - 1)
            moe()
            proj()
            for tb in range(2):
                norm_T(2, tb)
            ple()

            def wait_mix1(i, q):
                if i == 0 and q == 0:
                    pe.wait_ge(n_lo, nsplit(3, TB - 1, 1))
            dense(BLK["aq"], "w", before=wait_mix1)
            dense(BLK["aq"] + 1, "w")
            c = first_chunk(BLK["akv"])
            pe.wait_ge(lo_ready, c + 1)
            s = c % SPL
            for q in range(4):
                bank_read(BLK["akv"], q)
                parts = [(None, PS[0][:, :])] if q == 0 else [(q - 1, PS[q][:, 0:P])]
                if q == 3:
                    parts.append((3, PS[3][:, P:2 * P]))
                for tb, o in parts:
                    for kt in range(KT):
                        if tb is None:
                            w = slice(kt * 256, kt * 256 + P)
                            mm(o, whi[:, s, w], ahi[:, kt, :], kt == 0, False)
                            mm(o, whi[:, s, w], alo[:, kt, :], False, False)
                            last = mm(o, wlo[:, s, w], ahi[:, kt, :], False, kt == KT - 1)
                        else:
                            w = slice(kt * 256 + P, kt * 256 + 2 * P)
                            t_ = slice(tb * P, (tb + 1) * P)
                            mm(o, ahi[:, kt, t_], whi[:, s, w], kt == 0, False)
                            mm(o, ahi[:, kt, t_], wlo[:, s, w], False, False)
                            last = mm(o, alo[:, kt, t_], whi[:, s, w], False, kt == KT - 1)
                last.then_inc(w_used if q == 3 else d_done, 1)

            QT, KTa = area(AR_QT, 8, 512), area(AR_KT, P + SEQ)
            VN, PR, PTT = area(AR_VN, TB + 1, P), area(AR_PR, 2, 512), area(AR_PTT, 2, 512)
            UN = TB * 8

            def score(u):
                n, t = u // 8, u % 8
                if u == 0:
                    pe.wait_ge(t_v, 3)
                    pe.wait_ge(t_q, 9)
                    pe.wait_ge(t_pad, 2)
                if u >= 2:
                    pe.wait_ge(t_neg, u - 1)
                for hh in range(2):
                    r = slice(64 * hh, 64 * hh + 64)
                    o = PS[4 + u % 2 * 2 + hh]
                    last = mm(o[:, first_key(n):256], QT[r, t, n * P:(n + 1) * P],
                              KTa[r, n * P + first_key(n):(n + 2) * P], True, True)
                last.then_inc(t_s, 1)

            def prob_T(u):
                pe.wait_ge(t_e, 2 * u + 2)
                if u >= 2:
                    pe.wait_ge(t_pTc, u - 1)
                if u % 8 == 4 and u > 8:
                    pe.wait_ge(t_lo, 2 * (u // 8))
                for j in (range(4) if u >= 8 else (1, 3)):
                    last = nc.tensor.transpose(PS[2 + u % 2][:, j * P:(j + 1) * P],
                                               PR[:, u % 2, j * P:(j + 1) * P], ident)
                last.then_inc(t_pT, 1)

            def values(u):
                n, t = u // 8, u % 8
                pe.wait_ge(t_pTc, u + 1)
                if u == 0:
                    pe.wait_ge(t_v, 3)
                if t == 0 and n > 0:
                    pe.wait_ge(t_o, n)
                for hh in range(2):
                    first = first_key(n) // P
                    for kb in range(first, 2):
                        last = mm(PS[hh][:, t * HD:(t + 1) * HD],
                                  PTT[:, u % 2, (hh * 2 + kb) * P:(hh * 2 + kb + 1) * P],
                                  VN[:, n + kb, hh * HD:(hh + 1) * HD], kb == first, kb == 1)
                last.then_inc(t_pv, 1)

            def o_T(n):
                pe.wait_ge(t_o, n + 1)
                pe.wait_ge(t_pTc, min(8 * n + 12, UN))
                for half in range(2):
                    for t in range(4):
                        kt = half * 4 + t
                        last = nc.tensor.transpose(PS[2 + half][:, t * P:(t + 1) * P],
                                                   area(AR_AO, 2, D)[:, n % 2,
                                                                     kt * P:(kt + 1) * P], ident)
                    last.then_inc(t_oT, 1)

            score(0)
            score(1)
            for u in range(UN):
                prob_T(u)
                if u + 2 < UN:
                    score(u + 2)
                if u >= 1:
                    values(u - 1)
                if u % 8 == 3 and u > 8:
                    o_T(u // 8 - 1)
            values(UN - 1)
            o_T(TB - 1)

            def out1_before(i, q):
                if i == 0:
                    pe.wait_ge(t_lo, 2 * q + 2)
                    if q == 0:
                        pe.wait_ge(t_lo, 2 * TB)
            layer = 1
            dense(BLK["out1"], "act", before=out1_before)
            dense(BLK["out1"] + 1, "act", after=after_out(4))
            norm_T(4, TB - 1)
            router(TB - 2)
            router(TB - 1)
            moe()
            proj()
            for tb in range(2):
                norm_T(5, tb)
            ple()


        @block.scalar
        def _(act):
            todo = [0]
            chain = [0]

            def link(ins):
                chain[0] += 1
                ins.then_inc(a_link, 1)
                act.wait_ge(a_link, chain[0])

            def copy(o, i, scale=1.0):
                return nc.scalar.activation(o, i, ACT.Copy, scale=scale)

            def split(b, e6=0):
                if isinstance(e6, int):
                    act.wait_ge(w_full[b % RAW], 16 * (b // RAW + 1))
                    if b >= SPL:
                        act.wait_ge(w_used, b - SPL + 1)
                else:
                    act.wait_ge(w_full[b % RAW], e6 // 6 * 16 + 16 * (b // RAW + 1))
                    act.wait_ge(w_used, e6 + (b - SPL + 1))
                copy(whi[:, b % SPL, :], raw[:, b % RAW, :]).then_inc(hi_ready, 1)

            def splits(n):
                while todo[0] < min(n, NCHUNKS):
                    split(todo[0])
                    todo[0] += 1

            def root(n, tb):
                square(n, tb)
                sqrt(n, tb)

            def sqrt(n, tb):
                q = n * TB + tb
                nc.scalar.activation(st[:, q, 1:2], st[:, q, 0:1], ACT.Sqrt, bias=c_("eps"),
                                     scale=1.0 / D).then_inc(n_root, 1)

            def square(n, tb):
                q = n * TB + tb
                if n == 0:
                    act.wait_ge(s_x[tb], 16)
                    if tb == 0:
                        act.wait_ge(s_con, 16)
                else:
                    act.wait_ge(h_ready, (n - 1) * TB + tb + 1)
                    if n == 1 and tb == 0:
                        act.wait_ge(g_oT, TB)
                link(nc.scalar.activation(area(AR_JUNK, D), h[:, tb, :], ACT.Square,
                                          accum_out=st[:, q, 0:1]))

            def norm_hi(n, tb):
                q = n * TB + tb
                if n in FFN:
                    act.wait_ge(n_t, 2 * q + 1)
                    if tb >= 2:
                        act.wait_ge(M[FFN[n]]["rt"], tb - 1)
                    copy(area(AR_VT + tb % 2 * D, 512), PS[4][:, :]).then_inc(f_a, 1)
                    return
                for half in range(2):
                    act.wait_ge(n_t, 2 * q + half + 1)
                    copy(ahi[:, half * 4:half * 4 + 4, tb * P:(tb + 1) * P],
                         PS[4 + half][:, :].rearrange("p (a b) -> p a b", a=4)).then_inc(n_hi, 1)

            for tb in range(TB):
                root(0, tb)
                if tb == 0:
                    splits(1)
                if tb > 0:
                    norm_hi(0, tb - 1)
            norm_hi(0, TB - 1)
            splits(2)
            splits(3)
            act.wait_ge(s_hc, 32)
            lbl_, lb2 = area(AR_LBL, 3, AW), area(AR_LB, 2, AW)
            act.wait_ge(g_lb, 1)
            nc.scalar.activation(lbl_, lbl_, ACT.Exp).then_inc(g_lb, 1)
            F, K, E = area(AR_F, TB, 512), area(AR_K, TB, 512), area(AR_E, TB, 512)
            Q, V, G = area(AR_Q, TB, 512), area(AR_V, TB, 512), area(AR_G, TB, 512)
            et, yt = area(AR_ET, 512), area(AR_YT, 512)
            splits(4)
            for tb in range(TB):
                group_done(act, BLK["f"], tb)
                nc.scalar.activation(F[:, tb, :], PS[tb][:, :], ACT.Sigmoid).then_inc(g_sig, 1)
            splits(5)
            for tb in range(TB):
                act.wait_ge(g_k, tb + 1)
                nc.scalar.activation(F[:, tb, :], F[:, tb, :], ACT.Ln).then_inc(g_log, 1)
            dec = area(AR_DEC, 64)
            for tb in range(TB):
                if tb == 1:
                    splits(6)
                act.wait_ge(g_cum, tb + 1)
                if tb > 0:
                    act.wait_ge(g_kinv, tb)
                nc.scalar.activation(E[:, tb, :], PS[4][:, :], ACT.Exp).then_inc(g_eb, 1)
                nc.scalar.activation(et, PS[4][:, :], ACT.Exp, scale=-1.0).then_inc(g_enb, 1)
                if tb > 0:
                    act.wait_ge(g_ktail, tb)
                nc.scalar.activation(yt, PS[5][:, :], ACT.Exp).then_inc(g_esf, 1)
            nc.scalar.activation(dec, PS[6][:, 0:64], ACT.Exp).then_inc(g_dec, 1)
            splits(6)
            for tb in range(TB):
                group_done(act, BLK["q"], tb)
                nc.scalar.activation(Q[:, tb, :], PS[tb][:, :], ACT.Silu).then_inc(g_silu, 1)
            splits(7)
            splits(8)
            act.wait_ge(n_t, 2 * TB)
            for tb in range(TB):
                group_done(act, BLK["v"], tb)
                copy(V[:, tb, :], PS[tb][:, :]).then_inc(g_v, 1)
                act.wait_ge(g_kqT, 2 * tb + 2)
                copy(Q[:, tb, :], PS[6][:, :]).then_inc(g_QT, 1)
            splits(10)
            act.wait_ge(n_xn, TB)
            for tb in range(TB):
                group_done(act, BLK["g"], tb)
                nc.scalar.activation(G[:, tb, :], PS[tb][:, :], ACT.Sigmoid).then_inc(g_g, 1)

            def out_rows(tb):
                act.wait_ge(g_in, CPB * (tb + 1))
                copy(K[:, tb, :], PS[7][:, :]).then_inc(g_o, 1)

            def out_root(tb):
                act.wait_ge(g_osum, tb + 1)
                nc.scalar.activation(ssb[:, tb, 4:8], ssb[:, tb, 0:4], ACT.Sqrt, bias=c_("eps"),
                                     scale=1.0 / P).then_inc(g_oroot, 1)

            splits(11)
            splits(12)
            for q in range(4):
                group_done(act, BLK["C"], q)
                if q == 0:
                    act.wait_ge(g_qdec, TB)
                copy(E[:, q, :], PS[q][:, :]).then_inc(g_C, 1)
                if q == 0:
                    out_rows(0)
            out_root(0)
            splits(13)
            out_rows(1)
            splits(14)
            out_root(1)
            out_rows(2)
            out_root(2)
            splits(15)
            out_rows(3)
            splits(16)
            out_root(3)
            for ft in range(4):
                act.wait_ge(g_ob, ft + 1)
                if ft == 0:
                    act.wait_ge(w_used, first_chunk(BLK["out0"]))
                copy(ahi[:, 4 + ft, :], E[:, ft, :]).then_inc(g_bhi, 1)
            splits(17)
            for tb in range(TB):
                act.wait_ge(g_oT, tb + 1)
                copy(ahi[:, 0:4, tb * P:(tb + 1) * P],
                     PS[4 + tb % 2][:, :].rearrange("p (a b) -> p a b", a=4)).then_inc(g_mhi, 1)
            splits(18)

            def tail(n):
                for q in range(TB):
                    root(n, q)
                    if q > 0:
                        norm_hi(n, q - 1)
                norm_hi(n, TB - 1)

            def moe(layer):
                m = M[layer]
                B = MOE[layer]
                act.wait_ge(m["rtd"], 1)
                nc.scalar.activation(rtv("ex"), rtv("L"), ACT.Exp).then_inc(m["ex"], 1)

                def silu(e, b, e6):
                    act.wait_ge(w_used, e6 + (b + 2))
                    if not (isinstance(e, int) and e == 0):
                        act.wait_ge(m["hid"], e)
                    nc.scalar.activation(area(AR_SG, 512), PS[0][:, :], ACT.Silu)\
                      .then_inc(m["silu"], 1)

                def hid_hi(e):
                    act.wait_ge(m["hT"], e + 1)
                    copy(ahi[:, 0:4, P:2 * P],
                         PS[6][:, :].rearrange("p (a b) -> p a b", a=4)).then_inc(m["hhi"], 1)

                def x_hi(e):
                    for half in range(2):
                        act.wait_ge(m["xt"], 2 * e + (half + 1))
                        copy(ahi[:, half * 4:half * 4 + 4, 0:P],
                             PS[4 + half][:, :].rearrange("p (a b) -> p a b", a=4))\
                            .then_inc(m["xhi"], 1)

                def result(e, i, b, e6):
                    act.wait_ge(w_used, e6 + (b + i + 1))
                    if i == 0:
                        act.wait_ge(m["cw"], 2 * e + 2)
                        if not (isinstance(e, int) and e == 0):
                            act.wait_ge(m["sca"], 16 * e)
                    nc.scalar.activation(area(AR_OUT, 2, 512)[:, i, :], PS[2 + i][:, :], ACT.Copy,
                                         scale=curw[:, 0:1]).then_inc(m["ou"], 1)

                x_hi(0)

                def step(e, b, e6, prev=True, nx=True):
                    split(b + 2, e6)
                    split(b + 3, e6)
                    silu(e, b, e6)
                    if not prev:
                        x_hi(e + 1)
                        split(b + 4, e6)
                        split(b + 5, e6)
                        return
                    split(b + 4, e6)
                    hid_hi(e - 1)
                    split(b + 5, e6)
                    if nx:
                        x_hi(e + 1)
                    split(b + 6, e6)
                    result(e - 1, 0, b + 4, e6)
                    split(b + 7, e6)
                    result(e - 1, 1, b + 4, e6)

                step(0, B, 0, prev=False)
                step(1, B - 2 + 6, 0)
                with act.Fori(2, EXP - 2) as e:
                    step(e, B - 2, 6 * e)
                for e in (EXP - 2, EXP - 1):
                    step(e, B - 2 + 6 * e, 0, nx=e + 1 < EXP)
                todo[0] = B + MOE_CHUNKS
                hid_hi(EXP - 1)
                result(EXP - 1, 0, B + MOE_CHUNKS - 2, 0)
                result(EXP - 1, 1, B + MOE_CHUNKS - 2, 0)
                with more(act, layer):
                    further(X[layer])
                splits(B + MOE_CHUNKS + 2)

            def further(f):
                with act.Fori(0, PASSES) as j:
                    with act.Fori(0, EXP) as e:
                        t = j * EXP + e
                        act.wait_ge(f["pe"], 5 * t + 2)
                        for half in range(2):
                            copy(area(AR_VT, 2, 512)[:, half, :], PS[4 + half][:, :])\
                                .then_inc(f["act"], 1)
                        act.wait_ge(f["pe"], 5 * t + 3)
                        nc.scalar.activation(area(AR_SG, 512), PS[0][:, :], ACT.Silu)\
                          .then_inc(f["act"], 1)
                        act.wait_ge(f["pe"], 5 * t + 4)
                        copy(area(AR_VT + D, 512), PS[6][:, :]).then_inc(f["act"], 1)
                        act.wait_ge(f["pe"], 5 * t + 5)
                        act.wait_ge(f["dve"], 5 * t + 4)
                        for half in range(2):
                            nc.scalar.activation(area(AR_OUT, 2, 512)[:, half, :],
                                                 PS[2 + half][:, :], ACT.Copy,
                                                 scale=curw[:, 0:1]).then_inc(f["act"], 1)
                act.wait_ge(f["sca"], 16 * STEPS)

            def ple(layer):
                m = M[layer]
                n = 2 + 3 * layer
                k = BLK["ple0"] if layer == 0 else BLK["ple1"]
                act.wait_ge(m["sca"], 16 * EXP)
                for g in range(8):
                    act.wait_ge(m["pj"], g + 1)
                    copy(area(AR_PO, 8, 512)[:, g, :], PS[g % 4][:, :]).then_inc(m["pe"], 1)
                for tb in range(TB):
                    root(n, tb)
                    if tb > 0:
                        norm_hi(n, tb - 1)
                norm_hi(n, TB - 1)
                for i in range(2):
                    c = first_chunk(k + i)
                    splits(c + 3)
                    splits(c + 4)
                    for q in range(4):
                        g = i * 4 + q
                        group_done(act, k + i, q)
                        if 2 <= g < 6:
                            act.wait_ge(m["sg"], g - 1)
                        elif g >= 6:
                            act.wait_ge(h_ready, n * TB + g - 5)
                        elif g == 0:
                            act.wait_ge(m["pj"], 8)
                        nc.scalar.activation(area(AR_SIG + g % 2 * 512, 512), PS[q][:, :],
                                             ACT.Sigmoid).then_inc(m["gt"], 1)
                        if g > 4:
                            square(n + 1, q - 1)
                for tb in range(TB - 1):
                    sqrt(n + 1, tb)
                    if layer == 0 and tb > 0:
                        norm_hi(n + 1, tb - 1)
                square(n + 1, TB - 1)
                sqrt(n + 1, TB - 1)
                if layer == 0:
                    norm_hi(n + 1, TB - 2)
                    norm_hi(n + 1, TB - 1)

            splits(20)
            tail(1)
            moe(0)
            ple(0)

            QT, KTa = area(AR_QT, 8, 512), area(AR_KT, P + SEQ)
            for i in range(2):
                c = first_chunk(BLK["aq"] + i)
                splits(c + 4)
                for q in range(4):
                    group_done(act, BLK["aq"] + i, q)
                    if i == 0 and q == 0:
                        act.wait_ge(s_acon, 16)
                        act.wait_ge(h_ready, 3 * TB)
                    nc.scalar.activation(QT[:, i * 4 + q, :], PS[q][:, :], ACT.Identity,
                                         bias=ac("bq")[:, i * 4 + q:i * 4 + q + 1])\
                        .then_inc(t_q, 1)
            splits(first_chunk(BLK["akv"]) + 3)
            group_done(act, BLK["akv"], 0)
            nc.scalar.activation(KTa[:, P:], PS[0][:, :], ACT.Identity, bias=ac("bq")[:, 8:9])\
              .then_inc(t_q, 1)
            splits(first_chunk(BLK["akv"]) + 4)
            SM, PR, PTT = area(AR_SM, 2, 2, 256), area(AR_PR, 2, 2, 256), area(AR_PTT, 2, 512)
            ST2 = area(AR_ST2, 4, 64)

            def probs(u):
                act.wait_ge(t_sub, u + 1)
                if u >= 2:
                    act.wait_ge(t_pT, u - 1)
                a = first_key(u // 8)
                for hh in range(2):
                    j = u * 2 + hh
                    nc.scalar.activation(PR[:, u % 2, hh, a:], SM[:, u % 2, hh, a:], ACT.Exp,
                                         bias=ST2[:, 0, j:j + 1], accum_out=ST2[:, 1, j:j + 1])\
                      .then_inc(t_e, 1)

            def pT_copy(u):
                act.wait_ge(t_pT, u + 1)
                if u >= 2:
                    act.wait_ge(t_pv, u - 1)
                a = first_key(u // 8)
                copy(PTT[:, u % 2, :].rearrange("p (a b) -> p a b", a=2)[:, :, a:],
                     PS[2 + u % 2][:, :].rearrange("p (a b) -> p a b", a=2)[:, :, a:])\
                    .then_inc(t_pTc, 1)

            def sink_exp(n):
                act.wait_ge(t_den, 2 * n + 1)
                nc.scalar.activation(ST2[:, 2, n * 16:(n + 1) * 16],
                                     ST2[:, 2, n * 16:(n + 1) * 16], ACT.Exp).then_inc(t_den, 1)

            def o_hi(n):
                for half in range(2):
                    act.wait_ge(t_oT, 2 * n + half + 1)
                    copy(ahi[:, half * 4:half * 4 + 4, n * P:(n + 1) * P],
                         PS[2 + half][:, :].rearrange("p (a b) -> p a b", a=4)).then_inc(t_hi, 1)

            for u in range(8 * TB):
                probs(u)
                if u >= 1:
                    pT_copy(u - 1)
                if u % 8 == 7:
                    sink_exp(u // 8)
                if u % 8 == 4 and u > 8:
                    o_hi(u // 8 - 1)
            pT_copy(8 * TB - 1)
            o_hi(TB - 1)
            splits(MOE1 + 2)
            tail(4)
            moe(1)
            ple(1)

        @block.vector
        def _(dve):
            todo = [0]
            chain = [0]
            tt, ts, stt = nc.vector.tensor_tensor, nc.vector.tensor_scalar, \
                nc.vector.scalar_tensor_tensor

            def link(ins):
                chain[0] += 1
                ins.then_inc(v_link, 1)
                dve.wait_ge(v_link, chain[0])

            def split(b, e6=0):
                dve.wait_ge(hi_ready, e6 + (b + 1))
                if isinstance(e6, int):
                    dve.wait_ge(w_full[b % RAW], 16 * (b // RAW + 1))
                    if b >= SPL:
                        dve.wait_ge(w_used, b - SPL + 1)
                else:
                    dve.wait_ge(w_full[b % RAW], e6 // 6 * 16 + 16 * (b // RAW + 1))
                    dve.wait_ge(w_used, e6 + (b - SPL + 1))
                tt(wlo[:, b % SPL, :], raw[:, b % RAW, :], halves(whi[:, b % SPL, :]),
                   ALU.subtract).then_inc(lo_ready, 1)

            def splits(n):
                while todo[0] < min(n, NCHUNKS):
                    split(todo[0])
                    todo[0] += 1

            def norm_x(n, tb):
                q = n * TB + tb
                dve.wait_ge(n_root, q + 1)
                link(nc.vector.reciprocal(st[:, q, 2:3], st[:, q, 1:2]))
                if tb == 0:
                    dve.wait_ge(s_gain, 16 * (n + 1))
                if q >= 2 and n < 6:
                    dve.wait_ge(n_t, 2 * (q - 1))
                if n in FFN and tb >= 2:
                    dve.wait_ge(s_rows[tb - 2], 16 * FFN[n] + 16)
                if n == 1 and tb == 0:
                    dve.wait_ge(g_oT, TB)
                if n in (2, 5) and tb < 2:
                    dve.wait_ge(s_rows[tb + 2], 16 * (n // 3) + 16)
                if n == 4 and tb == 0:
                    dve.wait_ge(t_oT, 2 * TB)
                if n == 6 and tb < 2:
                    dve.wait_ge(n_t, 2 * 6 * TB)
                if n == 6 and tb >= 2:
                    dve.wait_ge(s_rows[tb - 2], 16 * LAYERS + 16)
                stt(xn(q), h[:, tb, :], st[:, q, 2:3], area(AR_GAIN, D), ALU.mult, ALU.mult)\
                    .then_inc(n_xn, 1)

            def norm_lo(n, tb):
                q = n * TB + tb
                if n in FFN:
                    dve.wait_ge(n_t, 2 * q + 2)
                    if tb >= 2:
                        dve.wait_ge(M[FFN[n]]["rt"], tb - 1)
                    nc.vector.tensor_copy(area(AR_VT + tb % 2 * D + 512, 512), PS[5][:, :])\
                      .then_inc(f_v, 1)
                    return
                for half in range(2):
                    dve.wait_ge(n_hi, nsplit(n, tb, half))
                    w = (slice(None), slice(half * 4, half * 4 + 4), slice(tb * P, (tb + 1) * P))
                    tt(alo[w], PS[4 + half][:, :].rearrange("p (a b) -> p a b", a=4),
                       halves(ahi[w]), ALU.subtract).then_inc(n_lo, 1)

            for tb in range(TB):
                norm_x(0, tb)
                if tb == 0:
                    splits(1)
                if tb > 0:
                    norm_lo(0, tb - 1)
            norm_lo(0, TB - 1)
            splits(2)
            lbl_, lb2 = area(AR_LBL, 3, AW), area(AR_LB, 2, AW)
            dve.wait_ge(s_hc, 32)
            mx = area(AR_ET, AW)
            link(tt(mx, lbl_[:, 0, :], lbl_[:, 1, :], ALU.max))
            link(tt(mx, mx, lbl_[:, 2, :], ALU.max))
            tt(lbl_, lbl_, mx.unsqueeze(1).to_broadcast([P, 3, AW]), ALU.subtract)\
                .then_inc(g_lb, 1)
            dve.wait_ge(g_lb, 2)
            link(tt(mx, lbl_[:, 0, :], lbl_[:, 1, :], ALU.add))
            link(tt(mx, mx, lbl_[:, 2, :], ALU.add))
            link(nc.vector.reciprocal(mx, mx))
            link(tt(lb2[:, 0, :], lbl_[:, 0, :], mx, ALU.mult))
            link(ts(lb2[:, 1, :], lb2[:, 0, :], -1.0, 1.0, ALU.mult, ALU.add))
            splits(4)
            F, K, E = area(AR_F, TB, 512), area(AR_K, TB, 512), area(AR_E, TB, 512)
            Q, V, G = area(AR_Q, TB, 512), area(AR_V, TB, 512), area(AR_G, TB, 512)
            et, yt = area(AR_ET, 512), area(AR_YT, 512)
            for tb in range(TB):
                dve.wait_ge(g_sig, tb + 1)
                link(tt(F[:, tb, :], F[:, tb, :], lb2[:, 1, :], ALU.mult))
                link(tt(F[:, tb, :], F[:, tb, :], lb2[:, 0, :], ALU.add))
                ts(K[:, tb, :], F[:, tb, :], -1.0, 1.0, ALU.mult, ALU.add).then_inc(g_k, 1)
            splits(5)
            for tb in range(TB):
                if tb == 1:
                    splits(6)
                dve.wait_ge(g_enb, tb + 1)
                dve.wait_ge(g_cum, tb + 1)
                tt(F[:, tb, :], K[:, tb, :], et, ALU.mult).then_inc(g_kinv, 1)
                dve.wait_ge(g_esf, tb + 1)
                tt(K[:, tb, :], K[:, tb, :], yt, ALU.mult).then_inc(g_ktail, 1)
            splits(6)
            S, ST = area(AR_S, HEADS, P), area(AR_ST, HEADS, P)
            nc.vector.memset(S, 0.0).then_inc(g_S, 1)
            for tb in range(TB):
                dve.wait_ge(g_silu, tb + 1)
                dve.wait_ge(g_eb, tb + 1)
                tt(Q[:, tb, :], Q[:, tb, :], E[:, tb, :], ALU.mult).then_inc(g_qdec, 1)
            splits(7)
            for tb in range(TB):
                dve.wait_ge(g_kqT, 2 * tb + 1)
                nc.vector.tensor_copy(F[:, tb, :], PS[7][:, :]).then_inc(g_KT, 1)
            dve.wait_ge(g_dec, 1)
            dec = area(AR_DEC, TB, HEADS, CPB)

            def rec(s):
                tb, r = s // 5, s % 5
                if tb < TB and r == 0:
                    dve.wait_ge(g_sc, tb + 1)
                    if tb > 0:
                        dve.wait_ge(g_in, CPB * (tb - 1) + 1)
                    tt(ST, PS[4][:, :].rearrange("p (a b) -> p a b", a=HEADS),
                       hc("triI").unsqueeze(1).to_broadcast([P, HEADS, P]), ALU.mult)\
                        .then_inc(g_scm, 1)
                n = tb * CPB + r - 1
                if tb < TB and r > 0 and n < NCH - 1:
                    dve.wait_ge(g_U, n + 1)
                    dve.wait_ge(g_in, n + 1)
                    for hh in range(HEADS):
                        last = stt(S[:, hh, :], S[:, hh, :], dec[:, tb, hh, n % CPB:n % CPB + 1],
                                   PS[5 + n % 2][:, hh * P:(hh + 1) * P], ALU.mult, ALU.add)
                    last.then_inc(g_S, 1)
                t = (s - 5) // 5
                if s >= 5 and s % 5 == 0:
                    dve.wait_ge(g_o, t + 1)
                    dve.wait_ge(g_sc, t + 1)
                    link(tt(F[:, t, :], K[:, t, :], K[:, t, :], ALU.mult))
                    nc.vector.tensor_reduce(ssb[:, t, 0:4],
                                            F[:, t, :].rearrange("p (a b) -> p a b", a=HEADS),
                                            AX, ALU.add).then_inc(g_osum, 1)
                if s >= 5 and s % 5 == 2:
                    dve.wait_ge(g_oroot, t + 1)
                    dve.wait_ge(g_g, TB)
                    link(nc.vector.reciprocal(ssb[:, t, 4:8], ssb[:, t, 4:8]))
                    k3 = K[:, t, :].rearrange("p (a b) -> p a b", a=HEADS)
                    link(tt(k3, k3, ssb[:, t, 4:8].unsqueeze(2).to_broadcast([P, HEADS, P]),
                            ALU.mult))
                    link(tt(k3, k3, hc("onorm").unsqueeze(1).to_broadcast([P, HEADS, P]),
                            ALU.mult))
                    tt(G[:, t, :], K[:, t, :], G[:, t, :], ALU.mult).then_inc(g_oa, 1)

            def conv(ft):
                w = hc("convw")[:, ft * 3:ft * 3 + 3]
                y = (yt, et)[ft % 2]
                if ft == 0:
                    dve.wait_ge(g_H, 4)
                    dve.wait_ge(g_kinv, TB)
                    dve.wait_ge(g_ktail, TB)
                if ft >= 2:
                    dve.wait_ge(g_ob, ft - 1)
                link(ts(y, E[:, ft, :], w[:, 2:3], None, ALU.mult))
                link(stt(y[:, 1:], E[:, ft, :SEQ - 1], w[:, 1:2], y[:, 1:], ALU.mult, ALU.add))
                link(stt(y[:, 2:], E[:, ft, :SEQ - 2], w[:, 0:1], y[:, 2:], ALU.mult, ALU.add))

            def gate(ft):
                group_done(dve, BLK["B"], ft)
                tt(E[:, ft, :], PS[ft][:, :], (yt, et)[ft % 2], ALU.mult).then_inc(g_ob, 1)

            splits(8)
            splits(9)
            splits(10)
            for b in range(3):
                for i in range(2):
                    splits(first_chunk(BLK["C"] + b) + i + 3)
                    for q in range(4):
                        if i == 1 and b == 1:
                            group_done(dve, BLK["H"], q)
                            dve.wait_ge(g_C, q + 1)
                            tt(E[:, q, :], PS[q][:, :], E[:, q, :], ALU.mult).then_inc(g_H, 1)
                        if i == 0 and b == 2 and q >= 2:
                            conv(q - 2)
                        if i == 1 and b == 2:
                            gate(q)
                            if q < 2:
                                conv(q + 2)
                        rec(b * 8 + i * 4 + q)
            for ft in range(4):
                dve.wait_ge(g_bhi, ft + 1)
                dve.wait_ge(g_ob, ft + 1)
                tt(alo[:, 4 + ft, :], E[:, ft, :], halves(ahi[:, 4 + ft, :]), ALU.subtract)\
                    .then_inc(g_blo, 1)
            splits(17)
            for tb in range(TB):
                dve.wait_ge(g_mhi, tb + 1)
                w = (slice(None), slice(0, 4), slice(tb * P, (tb + 1) * P))
                tt(alo[w], PS[4 + tb % 2][:, :].rearrange("p (a b) -> p a b", a=4),
                   halves(ahi[w]), ALU.subtract).then_inc(g_mlo, 1)

            def add_out(k, half, q, n):
                group_done(dve, k, q)
                if k == BLK["out0"]:
                    dve.wait_ge(s_x[q], 16)
                o = h[:, q, half * 512:(half + 1) * 512]
                tt(o, PS[q][:, :], o, ALU.add).then_inc(h_ready if half else s_add, 1)

            def out_proj(k, n):
                splits(first_chunk(k) + 3)
                splits(first_chunk(k) + 4)
                for q in range(TB):
                    add_out(k, 0, q, n)
                splits(first_chunk(k + 1) + 4)
                for q in range(TB):
                    add_out(k + 1, 1, q, n)
                    norm_x(n, q)
                    if q > 0:
                        norm_lo(n, q - 1)
                norm_lo(n, TB - 1)

            def moe(layer):
                m = M[layer]
                B = MOE[layer]
                v = {n: rtv(n) for n in RT}
                nc.vector.memset(v["info"], 0.0)
                link(nc.vector.memset(v["ones"], 1.0))

                def b3(x, k):
                    return x.unsqueeze(2).to_broadcast([P, x.shape[1], k])

                dve.wait_ge(m["rt"], TB)
                lg = PS[6][:, 0:TB * EXP].rearrange("p (a b) -> p a b", a=TB)
                link(nc.vector.tensor_reduce(v["mx"], lg, AX, ALU.max))
                tt(v["L"], lg, b3(v["mx"], EXP), ALU.subtract).then_inc(m["rtd"], 1)
                dve.wait_ge(m["ex"], 1)
                link(nc.vector.tensor_reduce(v["sm"], v["ex"], AX, ALU.add))
                link(nc.vector.reciprocal(v["rs"], v["sm"]))
                link(tt(v["sc"], v["ex"], b3(v["rs"], EXP), ALU.mult))

                def ranks(o, x, groups):
                    xj = x.unsqueeze(2).to_broadcast([P, groups, 4, 4])
                    xi = x.unsqueeze(3).to_broadcast([P, groups, 4, 4])
                    gt, eq = v["gt"][:, 0:groups], v["eq"][:, 0:groups]
                    tt(gt, xj, xi, ALU.is_gt)
                    link(tt(eq, xj, xi, ALU.is_equal))
                    tl = c_("tril").unsqueeze(1).to_broadcast([P, groups, 16])
                    e2 = eq.rearrange("p g i j -> p g (i j)")
                    link(tt(e2, e2, tl, ALU.mult))
                    link(tt(gt, gt, eq, ALU.add))
                    link(nc.vector.tensor_reduce(o, gt, AX, ALU.add))

                def by4(x):
                    return x.rearrange("p a (g i) -> p (a g) i", i=4)

                rank = by4(v["rank"])
                ranks(rank, by4(v["sc"]), 16)
                link(ts(v["in2"], v["rank"], 1.5, None, ALU.is_lt))
                link(tt(v["s2"], v["sc"], v["in2"], ALU.mult))
                gs = v["gs"].rearrange("p a g -> p (a g)")
                link(nc.vector.tensor_reduce(gs, by4(v["s2"]), AX, ALU.add))
                ranks(v["grank"], v["gs"], TB)
                link(ts(v["gsel"], v["grank"], 0.5, None, ALU.is_lt))
                gsel = v["gsel"].rearrange("p a g -> p (a g)")
                tt(by4(v["M"]), by4(v["in2"]), b3(gsel, 4), ALU.mult).then_inc(m["msk"], 1)
                rgs = v["rgs"].rearrange("p a g -> p (a g)")
                link(ts(rgs, gs, 1e-30, None, ALU.max))
                link(nc.vector.reciprocal(rgs, rgs))
                link(tt(rgs, rgs, gsel, ALU.mult))
                info = v["info"].rearrange("p a (e c) -> p a e c", c=4)
                w2 = v["w"]
                link(tt(by4(w2), by4(v["s2"]), b3(rgs, 4), ALU.mult))
                nc.vector.tensor_copy(info[:, :, :, 2], w2)
                tk = c_("tok").unsqueeze(2).to_broadcast([P, TB, EXP])
                ts(info[:, :, :, 0], tk, -FAR, None, ALU.add)
                link(ts(v["a"], v["rank"], float(SEQ), -FAR, ALU.mult, ALU.add))
                link(tt(info[:, :, :, 1], v["a"], tk, ALU.add))
                dve.wait_ge(m["rk"], 1)
                dve.wait_ge(m["msk"], 1)
                link(stt(v["a"], PS[7][:, 0:64].rearrange("p (a b) -> p a b", a=TB), 1.0, v["M"],
                         ALU.add, ALU.mult))
                ts(v["pos"], v["a"], -1.0, None, ALU.add).then_inc(m["ixe"], 1)
                dve.wait_ge(m["ixe"], 1)

                def onehot(e):
                    if not (isinstance(e, int) and e == 0):
                        dve.wait_ge(m["ix"], e)
                    tt(area(AR_OH, TB, P), iota.unsqueeze(1).to_broadcast([P, TB, P]),
                       v["pos"][:, :, bass.ds(e, 1)].to_broadcast([P, TB, P]), ALU.is_equal)\
                        .then_inc(m["oh"], 1)

                def index(e):
                    dve.wait_ge(m["ix"], e + 1)
                    if not (isinstance(e, int) and e == 0):
                        dve.wait_ge(m["ga"], 16 * e)
                    ts(cur[:, 0:1], PS[7][:, 0:1], FAR, None, ALU.add).then_inc(m["src"], 1)
                    nc.vector.tensor_copy(v["idx"][:, bass.ds(e * 4, 4)], PS[7][:, 0:4])\
                      .then_inc(m["ixe"], 1)

                def target(e):
                    if not (isinstance(e, int) and e == 0):
                        dve.wait_ge(m["sca"], 16 * e)
                    dve.wait_ge(m["ixe"], e + 2)
                    ts(cur[:, 1:2], v["idx"][:, bass.ds(e * 4 + 1, 1)], FAR, None, ALU.add)\
                        .then_inc(m["cw"], 1)
                    nc.vector.tensor_copy(curw[:, 0:1], v["idx"][:, bass.ds(e * 4 + 2, 1)])\
                      .then_inc(m["cw"], 1)

                def x_lo(e):
                    for half in range(2):
                        dve.wait_ge(m["xhi"], 2 * e + (half + 1))
                        w = (slice(None), slice(half * 4, half * 4 + 4), slice(0, P))
                        tt(alo[w], PS[4 + half][:, :].rearrange("p (a b) -> p a b", a=4),
                           halves(ahi[w]), ALU.subtract).then_inc(m["xlo"], 1)

                def hid(e, b, e6):
                    dve.wait_ge(m["silu"], e + 1)
                    dve.wait_ge(w_used, e6 + (b + 4))
                    if not (isinstance(e, int) and e == 0):
                        dve.wait_ge(m["hT"], e)
                    tt(area(AR_HID, 512), PS[1][:, :], area(AR_SG, 512), ALU.mult)\
                        .then_inc(m["hid"], 1)

                def hid_lo(e):
                    dve.wait_ge(m["hhi"], e + 1)
                    w = (slice(None), slice(0, 4), slice(P, 2 * P))
                    tt(alo[w], PS[6][:, :].rearrange("p (a b) -> p a b", a=4), halves(ahi[w]),
                       ALU.subtract).then_inc(m["hlo"], 1)

                onehot(0)
                dve.wait_ge(m["rk"], 2)
                link(nc.vector.tensor_reduce(v["cnt"][:, 0:1], PS[6][:, 64:64 + EXP], AX, ALU.max))
                ts(flag[:, layer:layer + 1], v["cnt"][:, 0:1], SLOTS + 0.5, None, ALU.is_gt)\
                    .then_inc(m["flg"], 1)
                index(0)
                onehot(1)
                index(1)
                x_lo(0)

                def step(e, b, e6, prev=True, nx=True, nx2=True):
                    split(b + 2, e6)
                    split(b + 3, e6)
                    if nx2:
                        onehot(e + 2)
                    if prev:
                        split(b + 4, e6)
                        hid_lo(e - 1)
                        target(e - 1)
                        split(b + 5, e6)
                    hid(e, b, e6)
                    if nx:
                        x_lo(e + 1)
                    if nx2:
                        index(e + 2)
                    split(b + (6 if prev else 4), e6)
                    split(b + (7 if prev else 5), e6)

                step(0, B, 0, prev=False)
                step(1, B - 2 + 6, 0)
                with dve.Fori(2, EXP - 2) as e:
                    step(e, B - 2, 6 * e)
                for e in (EXP - 2, EXP - 1):
                    step(e, B - 2 + 6 * e, 0, nx=e + 1 < EXP, nx2=False)
                todo[0] = B + MOE_CHUNKS
                hid_lo(EXP - 1)
                target(EXP - 1)
                with more(dve, layer):
                    further(m, X[layer], v)
                splits(B + MOE_CHUNKS + 2)

            def ple(layer):
                m = M[layer]
                n = 2 + 3 * layer
                k = BLK["ple0"] if layer == 0 else BLK["ple1"]

                def add_experts(tb):
                    dve.wait_ge(s_y[tb % 2], 16 * (tb // 2 + 1) + 32 * layer)
                    y = area(AR_YC + tb % 2 * CW, 2, D)
                    link(tt(h[:, tb, :], h[:, tb, :], y[:, 0, :], ALU.add))
                    tt(h[:, tb, :], h[:, tb, :], y[:, 1, :], ALU.add).then_inc(h_ready, 1)

                add_experts(0)
                for tb in range(TB):
                    if tb + 1 < TB:
                        add_experts(tb + 1)
                    norm_x(n, tb)
                    if tb > 0:
                        norm_lo(n, tb - 1)
                norm_lo(n, TB - 1)
                for i in range(2):
                    c = first_chunk(k + i)
                    splits(c + 3)
                    splits(c + 4)
                    for q in range(4):
                        g = i * 4 + q
                        dve.wait_ge(m["gt"], g + 1)
                        dve.wait_ge(m["pe"], 8)
                        if g == 0:
                            dve.wait_ge(m["pj"], 8)
                        sg = area(AR_SIG + g % 2 * 512, 512)
                        link(tt(sg, sg, area(AR_PO, 8, 512)[:, q * 2 + i, :], ALU.mult))
                        o = h[:, q, i * 512:(i + 1) * 512]
                        tt(o, o, sg, ALU.add).then_inc(h_ready if i else m["sg"], 1)
                for tb in range(TB):
                    norm_x(n + 1, tb)
                    if layer == 0 and tb > 0:
                        norm_lo(n + 1, tb - 1)
                if layer == 0:
                    norm_lo(n + 1, TB - 1)

            def further(m, f, v):
                dve.wait_ge(m["ix"], EXP)
                dve.wait_ge(m["sca"], 16 * EXP)
                dve.wait_ge(m["cw"], 2 * EXP)
                with dve.Fori(0, PASSES) as j:
                    ts(v["pos"], v["pos"], -float(SLOTS), None, ALU.add).then_inc(f["pos"], 1)
                    with dve.Fori(0, EXP) as e:
                        t = j * EXP + e
                        dve.wait_ge(f["pos"], j + 1)
                        tt(area(AR_OH, TB, P), iota.unsqueeze(1).to_broadcast([P, TB, P]),
                           v["pos"][:, :, bass.ds(e, 1)].to_broadcast([P, TB, P]), ALU.is_equal)\
                            .then_inc(f["dve"], 1)
                        dve.wait_ge(f["pe"], 5 * t + 1)
                        for i in range(2):
                            ts(cur[:, i:i + 1], PS[7][:, i:i + 1], FAR, None, ALU.add)\
                                .then_inc(f["dve"], 1)
                        nc.vector.tensor_copy(curw[:, 0:1], PS[7][:, 2:3]).then_inc(f["dve"], 1)
                        dve.wait_ge(f["act"], 6 * t + 3)
                        dve.wait_ge(f["pe"], 5 * t + 3)
                        tt(area(AR_HID, 512), PS[1][:, :], area(AR_SG, 512), ALU.mult)\
                            .then_inc(f["dve"], 1)
                        dve.wait_ge(f["sca"], 16 * t + 16)
                    dve.wait_ge(f["dve"], (j + 1) * (5 * EXP))

            out_proj(BLK["out0"], 1)
            moe(0)
            ple(0)

            VN, SM = area(AR_VN, TB + 1, P), area(AR_SM, 2, 512)
            ST2 = area(AR_ST2, 4, 64)
            nc.vector.memset(area(AR_KT, P + SEQ)[:, 0:P], 0.0).then_inc(t_pad, 1)
            nc.vector.memset(VN[:, 0, :], 0.0).then_inc(t_pad, 1)
            dve.wait_ge(s_acon, 16)
            ts(ST2[:, 3, 0:16], ac("sink"), -1.0, None, ALU.mult).then_inc(t_pad, 1)
            for i in range(2):
                splits(first_chunk(BLK["aq"] + i) + 4)
            splits(first_chunk(BLK["akv"]) + 3)
            for q in range(1, 4):
                group_done(dve, BLK["akv"], q)
                for tb, col in ([(q - 1, 0)] if q < 3 else [(2, 0), (3, P)]):
                    last = tt(VN[:, tb + 1, :], PS[q][:, col:col + P], ac("bv"), ALU.add)
                last.then_inc(t_v, 1)
            splits(first_chunk(BLK["akv"]) + 4)
            dve.wait_ge(t_pad, 3)

            def scale_mask(u):
                dve.wait_ge(t_s, u + 1)
                if u >= 2:
                    dve.wait_ge(t_e, 2 * (u - 1))
                mk = ac("mask")[:, 0:256] if u < 8 else ac("mask")[:, 256:512]
                a = first_key(u // 8)
                sm = SM[:, u % 2, :].rearrange("p (a b) -> p a b", a=2)[:, :, a:]
                stt(sm, psum[:, 4 + u % 2 * 2:6 + u % 2 * 2, a:256], HD ** -0.5,
                    mk[:, a:].unsqueeze(1).to_broadcast([P, 2, 256 - a]), ALU.mult, ALU.add)\
                    .then_inc(t_neg, 1)
                dve.wait_ge(t_neg, u + 1)
                nm = ST2[:, 0, 2 * u:2 * u + 2]
                link(nc.vector.tensor_reduce(nm, sm, AX, ALU.max, negate=True))
                t = u % 8
                tt(nm, nm, ST2[:, 3, 2 * t:2 * t + 2], ALU.min).then_inc(t_sub, 1)
                if t == 7:
                    n = u // 8
                    dve.wait_ge(t_sub, u + 1)
                    tt(ST2[:, 2, n * 16:n * 16 + 16], ac("sink"), ST2[:, 0, n * 16:n * 16 + 16],
                       ALU.add).then_inc(t_den, 1)

            def finish(n):
                dve.wait_ge(t_e, 16 * (n + 1))
                dve.wait_ge(t_den, 2 * n + 2)
                dn = ST2[:, 1, n * 16:n * 16 + 16]
                link(tt(dn, dn, ST2[:, 2, n * 16:n * 16 + 16], ALU.add))
                link(nc.vector.reciprocal(dn, dn))
                dve.wait_ge(t_pv, 8 * (n + 1))
                if n >= 2:
                    dve.wait_ge(t_oT, 2 * (n - 1))
                d2 = dn.rearrange("p (t a) -> p t a", a=2)
                for hh in range(2):
                    o = area(AR_AO, 2, 2, 512)[:, n % 2, hh, :].rearrange("p (t c) -> p t c", t=8)
                    last = tt(o, PS[hh][:, :].rearrange("p (t c) -> p t c", t=8),
                              d2[:, :, hh:hh + 1].to_broadcast([P, 8, HD]), ALU.mult)
                last.then_inc(t_o, 1)

            def o_lo(n):
                for half in range(2):
                    dve.wait_ge(t_hi, 2 * n + half + 1)
                    w = (slice(None), slice(half * 4, half * 4 + 4), slice(n * P, (n + 1) * P))
                    tt(alo[w], PS[2 + half][:, :].rearrange("p (a b) -> p a b", a=4),
                       halves(ahi[w]), ALU.subtract).then_inc(t_lo, 1)

            for u in range(8 * TB):
                scale_mask(u)
                if u % 8 == 1 and u > 8:
                    finish(u // 8 - 1)
                if u % 8 == 4 and u > 8:
                    o_lo(u // 8 - 1)
            finish(TB - 1)
            o_lo(TB - 1)
            dve.wait_ge(t_bo, 16)
            for tb in range(TB):
                last = tt(h[:, tb, :], h[:, tb, :], area(AR_BO, D), ALU.add)
            link(last)
            out_proj(BLK["out1"], 4)
            moe(1)
            ple(1)

        @block.gpsimd
        def _(pool):
            def gain(n):
                if n > 0:
                    pool.wait_ge(n_xn, TB * n)
                if n == 1:
                    pool.wait_ge(g_oT, TB)
                pool.dma_start(area(AR_GAIN, D), gains[n]).then_inc(s_gain, 16)

            last_row, last_target = pool.to_reg(SEQ - 1), pool.to_reg(2 * SEQ - 1)
            gain(0)
            pool.dma_start(ar[:, AR_HC:AR_HC + HCONST_N], hconsts).then_inc(s_hc, 16)
            pool.dma_start(area(AR_LBL, 3, AW), lbl).then_inc(s_hc, 16)
            gain(1)
            for layer in range(LAYERS):
                m = M[layer]
                if layer == 1:
                    pool.wait_ge(t_lo, 2 * TB)
                else:
                    pool.wait_ge(g_mlo, TB)
                    pool.wait_ge(g_blo, TB)
                nc.gpsimd.memset(area(AR_XG, D), 0.0).then_inc(m["xz"], 1)
                pool.dma_start(area(AR_PT, 2, SEQ), pT[layer]).then_inc(m["pl"], 16)
                pool.dma_start(area(AR_PW, 2, D), w_proj[layer]).then_inc(m["pl"], 16)
                n = 1 + 3 * layer
                for tb in range(TB):
                    pool.wait_ge(n_xn, n * TB + tb + 1)
                    pool.dma_start(vscr[layer][tb * P:(tb + 1) * P, :], xn(n * TB + tb))\
                        .then_inc(s_rows[tb], 16)
                gain(n + 1)

                def ready(*waits):
                    for s, n in waits:
                        pool.wait_ge(s, n)
                    pool.sem_inc(p_ready, 1)

                def gather(e):
                    if isinstance(e, int) and e == 0:
                        for tb in range(TB):
                            pool.wait_ge(s_rows[tb], 16 * layer + 16)
                        pool.wait_ge(m["xz"], 1)
                        ready((m["src"], 1))
                    else:
                        ready((m["src"], e + 1),
                              (m["xt"], 2 * e))
                    nc.gpsimd.indirect_dma_start(
                        out=area(AR_XG, D), out_offset=None, in_=vscr[layer],
                        in_offset=bass.IndirectOffsetOnAxis(ap=cur[:, 0:1], axis=0),
                        bounds_check=last_row, oob_is_err=False).then_inc(m["ga"], 16)

                def scatter(e):
                    ready((m["ou"], 2 * e + 2),
                          (m["cw"], 2 * e + 2))
                    nc.gpsimd.indirect_dma_start(
                        out=yscr[layer],
                        out_offset=bass.IndirectOffsetOnAxis(ap=cur[:, 1:2], axis=0),
                        in_=area(AR_OUT, D), in_offset=None,
                        bounds_check=last_target, oob_is_err=False).then_inc(m["sca"], 16)

                gather(0)
                gather(1)
                gather(2)
                scatter(0)
                gather(3)
                with pool.Fori(2, EXP - 2) as e:
                    scatter(e - 1)
                    gather(e + 2)
                for e in range(EXP - 2, EXP + 1):
                    scatter(e - 1)
                pool.wait_ge(m["sca"], 16 * EXP)
                with more(pool, layer):
                    f = X[layer]
                    with pool.Fori(0, PASSES) as j:
                        with pool.Fori(0, EXP) as e:
                            t = j * EXP + e
                            ready((f["dve"], 5 * t + 4))
                            nc.gpsimd.indirect_dma_start(
                                out=area(AR_XG, D), out_offset=None, in_=vscr[layer],
                                in_offset=bass.IndirectOffsetOnAxis(ap=cur[:, 0:1], axis=0),
                                bounds_check=last_row, oob_is_err=False).then_inc(f["ga"], 16)
                            ready((f["act"], 6 * t + 6))
                            nc.gpsimd.indirect_dma_start(
                                out=yscr[layer],
                                out_offset=bass.IndirectOffsetOnAxis(ap=cur[:, 1:2], axis=0),
                                in_=area(AR_OUT, D), in_offset=None,
                                bounds_check=last_target, oob_is_err=False)\
                                .then_inc(f["sca"], 16)
                    pool.wait_ge(f["sca"], 16 * STEPS)
                for tb in range(TB):
                    if tb >= 2:
                        pool.wait_ge(h_ready, (n * TB) + tb - 1)
                    pool.dma_start(area(AR_YC + tb % 2 * CW, 2, D),
                                   yscr[layer].rearrange("(k t) d -> t k d", k=2)
                                   [tb * P:(tb + 1) * P, :, :])\
                        .then_inc(s_y[tb % 2], 16)
                gain(n + 2)
                if layer == 0:
                    pool.wait_ge(h_ready, 2 * TB)
                    pool.dma_start(ar[:, AR_AC:AR_AC + ACONST_N], aconsts).then_inc(s_acon, 16)
                    gain(4)
                    pool.wait_ge(t_s, 8 * TB)
                    pool.dma_start(area(AR_BO, D), bout).then_inc(t_bo, 16)
            for tb in range(TB):
                pool.wait_ge(n_xn, 6 * TB + tb + 1)
                pool.dma_start(out[tb * P:(tb + 1) * P, :], xn(6 * TB + tb)).then_inc(s_rows[tb], 16)
            for tb in range(TB):
                pool.wait_ge(s_rows[tb], 16 * LAYERS + 16)


def kernel(x, p, norm_mix, norm_ffn, norm_ple, norm_final, w_in_ab, hgrn_lb_logits,
           hgrn_out_norm, conv_w, w_out_ab, w_in_c, b_in_c, sinks, w_out_c, b_out_c,
           w_router, w_gate_e, w_up_e, w_down_e, w_ple_gate, w_ple_proj):
    import concourse.bacc as _bacc
    from concourse import mybir as _mybir
    from concourse.bass_utils import run_bass_kernel_spmd as _run

    A = np.asarray

    def rows(v):
        v = A(v).reshape(1, -1)
        return np.broadcast_to(v, (P, v.shape[1]))

    def cat(*a):
        return np.ascontiguousarray(np.concatenate(a, axis=-1))

    def blocks(w, order=(0, 1), n=512):
        w = A(w)
        k, cols = w.shape
        w = w.reshape(k // 512, 4, P, cols // n, n).transpose(3, 0, 2, 1, 4)
        return w[:, list(order)[:k // 512]].reshape(-1, P, 4 * n)

    def features(v):
        return A(v).reshape(-1, P).T

    i = np.arange(P)
    same = (i[:, None] // CHUNK) == (i[None, :] // CHUNK)
    consts = cat(np.eye(P, dtype=np.float32),
                 np.triu(np.ones((P, P), np.float32), 1),
                 np.broadcast_to(np.arange(P, dtype=np.float32), (P, P)),
                 np.arange(SEQ, dtype=np.float32).reshape(TB, P).T,
                 A(w_router).reshape(KT, P, EXP).transpose(1, 0, 2).reshape(P, -1),
                 np.broadcast_to(np.tril(np.ones((4, 4), np.float32), -1).reshape(1, 16), (P, 16)),
                 np.full((P, 1), EPS, np.float32))
    hconsts = cat((same & (i[:, None] <= i[None, :])).astype(np.float32),
                  (same & (i[:, None] > i[None, :])).astype(np.float32),
                  ((i[:, None] // CHUNK) == np.arange(CPB)[None, :]).astype(np.float32),
                  rows(hgrn_out_norm[0]),
                  A(conv_w)[0].reshape(3, 4, P).transpose(2, 1, 0).reshape(P, 12))
    qi, si = np.arange(P)[:, None] + P, np.arange(2 * P)[None, :]
    band = (qi - si >= 0) & (qi - si < P)
    masks = [np.where(band & (si >= P), 0, NEG), np.where(band, 0, NEG)]
    pair = np.arange(QH).reshape(2, 8).T.reshape(-1)
    bi = A(b_in_c)[0]
    bq = bi[:D].reshape(QH, HD)[pair].reshape(8, P)
    bk = bi[D:D + P].reshape(1, P)
    aconsts = cat(*(a.astype(np.float32) for a in masks),
                  np.concatenate([bq, bk]).T, rows(bi[D + P:]), rows(A(sinks)[0][pair]))
    gains = np.ascontiguousarray(np.stack([
        rows(g) for g in (norm_mix[0], norm_ffn[0], norm_ple[0], norm_mix[1], norm_ffn[1],
                          norm_ple[1], norm_final)]))
    lbl = np.ascontiguousarray(rows(hgrn_lb_logits)).reshape(P, 3, AW)
    wab = A(w_in_ab)[0]
    part = {n: wab[:, j * AW:(j + 1) * AW] for j, n in enumerate(("q", "f", "v", "g", "B", "C", "H"))}
    wc = A(w_in_c)[0]
    wq = wc[:, :D].reshape(D, QH, HD)[:, pair].reshape(D, D)
    wkv = wc[:, D:].reshape(KT, P, 256).transpose(1, 0, 2).reshape(1, P, CW)
    w_dense = np.ascontiguousarray(np.concatenate(
        [blocks(part[n]) for n in ("f", "q", "v", "g", "C", "H", "B")] +
        [blocks(A(w_out_ab)[0], (1, 0)), blocks(A(w_ple_gate)[0]), blocks(wq), wkv,
         blocks(A(w_out_c)[0]), blocks(A(w_ple_gate)[1])]))

    def experts(layer):
        return np.stack([np.concatenate([blocks(A(w)[layer, e])
                                         for w in (w_gate_e, w_up_e, w_down_e)])
                         for e in range(EXP)]).reshape(MOE_CHUNKS, P, CW)

    w_moe = np.ascontiguousarray(np.stack([experts(layer) for layer in range(LAYERS)]))
    w_proj = np.ascontiguousarray(A(w_ple_proj).reshape(LAYERS, 2, P, D).transpose(0, 2, 1, 3))
    pT = np.ascontiguousarray(A(p)[:, 0].reshape(LAYERS, SEQ, 2, P).transpose(0, 3, 2, 1))
    data = {"consts": consts, "hconsts": hconsts, "aconsts": aconsts, "gains": gains, "lbl": lbl,
            "bout": np.ascontiguousarray(rows(A(b_out_c)[0])), "x": np.ascontiguousarray(A(x)[0]),
            "pT": pT, "w_dense": w_dense, "w_moe": w_moe, "w_proj": w_proj}

    nc = _bacc.Bacc("TRN2", target_bir_lowering=False, num_devices=1)
    f32 = _mybir.dt.float32
    aps = {n: nc.dram_tensor(n + "_dram", a.shape, f32, kind="ExternalInput").ap()
           for n, a in data.items()}
    aps["out"] = nc.dram_tensor("out_dram", (SEQ, D), f32, kind="ExternalOutput").ap()
    aps["vscr"] = [nc.dram_tensor(f"vscr{j}", (SEQ, D), f32).ap() for j in range(LAYERS)]
    aps["yscr"] = [nc.dram_tensor(f"yscr{j}", (2 * SEQ, D), f32).ap() for j in range(LAYERS)]
    build(nc, **aps)
    r = _run(nc, [{n + "_dram": a for n, a in data.items()}], core_ids=[0])
    return r.results[0]["out_dram"].reshape(1, SEQ, D)
```
